# Optimizing a Trainium2 kernel written in Bass

```python
import math
import jax, jax.numpy as jnp
from jax import lax
import numpy as np

'''Hybrid streaming-encoder trunk (chunk-causal; all mixers here are frame-causal).

Each of the DEPTH post-norm (DeepNorm) layers computes
  x <- LN(alpha*x + 0.5*SwiGLU_1(x))                                  macaron half-step FFN
  x <- LN(alpha*x + W_out[ RMS(RG-LRU) | RMS(FoX attn) | RMS(S5+GLU) ])  parallel head groups
  x <- LN(alpha*x + 0.5*SwiGLU_2(x))                                  macaron half-step FFN
with one combined input projection whose columns are partitioned among the three mixers.
Input  x: (BATCH, SEQ, D_MODEL) float32.
Output y: (BATCH, SEQ, D_MODEL).
'''

D_MODEL = 1024
BATCH = 1
SEQ = 256
DEPTH = 2

CHUNK = 64
D_MIX = D_MODEL
D_A = 3 * D_MIX // 8
A_BLOCK_DIM = 64
A_BLOCKS = D_A // A_BLOCK_DIM
CONV_WIDTH = 4
RG_C = 8.0
B_HEAD_DIM = 64
D_B = 3 * D_MIX // 8
B_HEADS = D_B // B_HEAD_DIM
Q_BLOCK = 128
D_C = D_MIX - D_A - D_B
C_GROUP = 16
C_GROUPS = D_C // C_GROUP
C_STATE = 64
N_IN = 2 * D_A + 3 * D_B + B_HEADS + D_C
D_FF = 2816
ALPHA = (2 * DEPTH) ** 0.25
BETA = (8 * DEPTH) ** -0.25
LN_EPS = 1e-5
RMS_EPS = 1e-6

kernel_name = "hybrid_rglru_fox_s5_macaron_deepnorm"

def layer_norm(x, g, b):
    xf = x.astype(jnp.float32)
    mu = jnp.mean(xf, axis=-1, keepdims=True)
    var = jnp.mean(jnp.square(xf - mu), axis=-1, keepdims=True)
    return ((xf - mu) * lax.rsqrt(var + LN_EPS) * g + b).astype(x.dtype)

def rms_norm(x, g):
    xf = x.astype(jnp.float32)
    return xf * lax.rsqrt(jnp.mean(xf * xf, axis=-1, keepdims=True) + RMS_EPS) * g

def swiglu(x, w_gate, w_up, w_down):
    return (jax.nn.silu(x @ w_gate) * (x @ w_up)) @ w_down

def causal_depthwise_conv(x, w, b):
    s = x.shape[1]
    xp = jnp.pad(x, ((0, 0), (CONV_WIDTH - 1, 0), (0, 0)))
    out = b
    for k in range(CONV_WIDTH):
        out = out + w[k] * xp[:, k:k + s]
    return out

def linear_scan(a, b):
    def combine(left, right):
        a_l, b_l = left
        a_r, b_r = right
        return a_l * a_r, a_r * b_l + b_r
    return lax.associative_scan(combine, (a, b), axis=1)[1]

def rg_lru(x, w_a, b_a, w_x, b_x, lam):
    bsz, s, _ = x.shape
    xb = x.reshape(bsz, s, A_BLOCKS, A_BLOCK_DIM)
    r = jax.nn.sigmoid(jnp.einsum('bshi,hij->bshj', xb, w_a).reshape(bsz, s, D_A) + b_a)
    i = jax.nn.sigmoid(jnp.einsum('bshi,hij->bshj', xb, w_x).reshape(bsz, s, D_A) + b_x)
    log_a = -RG_C * r * jax.nn.softplus(-lam)
    a = jnp.exp(log_a)
    gated = jnp.sqrt(-jnp.expm1(2.0 * log_a)) * (i * x)
    return linear_scan(a, gated)

def forgetting_attention(q, k, v, log_f):
    s = q.shape[2]
    scale = B_HEAD_DIM ** -0.5
    c = jnp.cumsum(log_f, axis=-1)
    outs = []
    for blk in range(s // Q_BLOCK):
        q0 = blk * Q_BLOCK
        q1 = q0 + Q_BLOCK
        qb = q[:, :, q0:q1]
        kb = k[:, :, :q1]
        vb = v[:, :, :q1]
        logits = jnp.einsum('bhqd,bhkd->bhqk', qb, kb) * scale
        logits = logits + (c[:, :, q0:q1, None] - c[:, :, None, :q1])
        mask = (q0 + jnp.arange(Q_BLOCK))[:, None] >= jnp.arange(q1)[None, :]
        logits = jnp.where(mask, logits, -jnp.inf)
        p = jax.nn.softmax(logits, axis=-1)
        outs.append(jnp.einsum('bhqk,bhkd->bhqd', p, vb))
    return jnp.concatenate(outs, axis=2)

def s5_ssm(u, a_re, a_im, log_dt, b_re, b_im, c_re, c_im, d, w_glu):
    f32 = jnp.float32
    bsz, s, _ = u.shape
    lam = lax.complex(a_re.astype(f32), a_im.astype(f32))
    dt = jnp.exp(log_dt.astype(f32))[:, None]
    a_bar = jnp.exp(lam * dt)
    b_bar = ((a_bar - 1.0) / lam)[:, :, None] * lax.complex(b_re.astype(f32), b_im.astype(f32))
    c_mat = lax.complex(c_re.astype(f32), c_im.astype(f32))
    ug = u.astype(f32).reshape(bsz, s, C_GROUPS, C_GROUP)
    bu = jnp.einsum('bsgc,gpc->bsgp', ug.astype(jnp.complex64), b_bar)
    a_seq = jnp.broadcast_to(a_bar, (1, s, C_GROUPS, C_STATE))
    h = linear_scan(a_seq, bu)
    y = jnp.einsum('bsgp,gcp->bsgc', h, c_mat).real + d.astype(f32).reshape(C_GROUPS, C_GROUP) * ug
    y = jax.nn.gelu(y.reshape(bsz, s, D_C))
    return y * jax.nn.sigmoid(y @ w_glu.astype(f32))

def hybrid_mixer(x, w_in, conv_w, conv_b, rg_w_a, rg_b_a, rg_w_x, rg_b_x, rg_lambda, fox_b_f,
                 s5_a_re, s5_a_im, s5_log_dt, s5_b_re, s5_b_im, s5_c_re, s5_c_im, s5_d, s5_w_glu,
                 mix_norm_g, w_out):
    f32 = jnp.float32
    bsz, s, _ = x.shape
    z = x @ w_in
    cuts = [int(v) for v in np.cumsum([D_A, D_A, D_B, D_B, D_B, B_HEADS])]
    a_x, a_gate, q, k, v, f_logit, c_u = jnp.split(z, cuts, axis=-1)

    xa = causal_depthwise_conv(a_x, conv_w, conv_b).astype(f32)
    out_a = jax.nn.gelu(a_gate.astype(f32)) * rg_lru(xa, rg_w_a, rg_b_a, rg_w_x, rg_b_x, rg_lambda)

    def heads(t):
        return t.astype(f32).reshape(bsz, s, B_HEADS, B_HEAD_DIM).transpose(0, 2, 1, 3)
    log_f = jax.nn.log_sigmoid(f_logit.astype(f32) + fox_b_f).transpose(0, 2, 1)
    out_b = forgetting_attention(heads(q), heads(k), heads(v), log_f)
    out_b = out_b.transpose(0, 2, 1, 3).reshape(bsz, s, D_B)

    out_c = s5_ssm(c_u, s5_a_re, s5_a_im, s5_log_dt, s5_b_re, s5_b_im, s5_c_re, s5_c_im, s5_d, s5_w_glu)

    g_a, g_b, g_c = jnp.split(mix_norm_g, [D_A, D_A + D_B])
    o = jnp.concatenate([rms_norm(out_a, g_a), rms_norm(out_b, g_b), rms_norm(out_c, g_c)], axis=-1)
    return o.astype(x.dtype) @ w_out

def setup_inputs(seed: int = 0) -> dict:
    key = jax.random.key(seed)
    ks = jax.random.split(key, 40)
    L = DEPTH
    f32 = jnp.float32

    def nrm(k, shape, scale):
        return scale * jax.random.normal(k, shape, f32)

    u_a = jax.random.uniform(ks[11], (L, D_A), f32, minval=0.9, maxval=0.999)
    a0 = u_a ** (1.0 / RG_C)
    rg_lambda = jnp.log(a0) - jnp.log1p(-a0)
    s5_a_im = jnp.pi * jnp.arange(C_STATE, dtype=f32)[None, None, :] + nrm(ks[14], (L, C_GROUPS, C_STATE), 0.01)
    s5_log_dt = jax.random.uniform(ks[15], (L, C_GROUPS), f32, minval=math.log(1e-3), maxval=math.log(1e-1))
    return {
        'x': jax.random.normal(ks[0], (BATCH, SEQ, D_MODEL), f32),
        'ffn1_w_gate': nrm(ks[1], (L, D_MODEL, D_FF), D_MODEL ** -0.5),
        'ffn1_w_up': nrm(ks[2], (L, D_MODEL, D_FF), D_MODEL ** -0.5),
        'ffn1_w_down': nrm(ks[3], (L, D_FF, D_MODEL), BETA * D_FF ** -0.5),
        'ln1_g': 1.0 + nrm(ks[4], (L, D_MODEL), 0.02),
        'ln1_b': nrm(ks[5], (L, D_MODEL), 0.02),
        'w_in': nrm(ks[6], (L, D_MODEL, N_IN), D_MODEL ** -0.5),
        'conv_w': nrm(ks[7], (L, CONV_WIDTH, D_A), CONV_WIDTH ** -0.5),
        'conv_b': nrm(ks[8], (L, D_A), 0.02),
        'rg_w_a': nrm(ks[9], (L, A_BLOCKS, A_BLOCK_DIM, A_BLOCK_DIM), A_BLOCK_DIM ** -0.5),
        'rg_b_a': nrm(ks[10], (L, D_A), 0.02),
        'rg_w_x': nrm(ks[12], (L, A_BLOCKS, A_BLOCK_DIM, A_BLOCK_DIM), A_BLOCK_DIM ** -0.5),
        'rg_b_x': nrm(ks[16], (L, D_A), 0.02),
        'rg_lambda': rg_lambda,
        'fox_b_f': 2.0 + nrm(ks[17], (L, B_HEADS), 0.1),
        's5_a_re': -0.5 + nrm(ks[13], (L, C_GROUPS, C_STATE), 0.01),
        's5_a_im': s5_a_im,
        's5_log_dt': s5_log_dt,
        's5_b_re': nrm(ks[18], (L, C_GROUPS, C_STATE, C_GROUP), (2 * C_GROUP) ** -0.5),
        's5_b_im': nrm(ks[19], (L, C_GROUPS, C_STATE, C_GROUP), (2 * C_GROUP) ** -0.5),
        's5_c_re': nrm(ks[20], (L, C_GROUPS, C_GROUP, C_STATE), (2 * C_STATE) ** -0.5),
        's5_c_im': nrm(ks[21], (L, C_GROUPS, C_GROUP, C_STATE), (2 * C_STATE) ** -0.5),
        's5_d': nrm(ks[22], (L, D_C), 1.0),
        's5_w_glu': nrm(ks[23], (L, D_C, D_C), D_C ** -0.5),
        'mix_norm_g': 1.0 + nrm(ks[24], (L, D_MIX), 0.02),
        'w_out': nrm(ks[25], (L, D_MIX, D_MODEL), BETA * D_MIX ** -0.5),
        'ln2_g': 1.0 + nrm(ks[26], (L, D_MODEL), 0.02),
        'ln2_b': nrm(ks[27], (L, D_MODEL), 0.02),
        'ffn2_w_gate': nrm(ks[28], (L, D_MODEL, D_FF), D_MODEL ** -0.5),
        'ffn2_w_up': nrm(ks[29], (L, D_MODEL, D_FF), D_MODEL ** -0.5),
        'ffn2_w_down': nrm(ks[30], (L, D_FF, D_MODEL), BETA * D_FF ** -0.5),
        'ln3_g': 1.0 + nrm(ks[31], (L, D_MODEL), 0.02),
        'ln3_b': nrm(ks[32], (L, D_MODEL), 0.02),
    }

def reference(x, ffn1_w_gate, ffn1_w_up, ffn1_w_down, ln1_g, ln1_b,
              w_in, conv_w, conv_b, rg_w_a, rg_b_a, rg_w_x, rg_b_x, rg_lambda, fox_b_f,
              s5_a_re, s5_a_im, s5_log_dt, s5_b_re, s5_b_im, s5_c_re, s5_c_im, s5_d, s5_w_glu,
              mix_norm_g, w_out, ln2_g, ln2_b,
              ffn2_w_gate, ffn2_w_up, ffn2_w_down, ln3_g, ln3_b):
    for l in range(DEPTH):
        x = layer_norm(ALPHA * x + 0.5 * swiglu(x, ffn1_w_gate[l], ffn1_w_up[l], ffn1_w_down[l]),
                       ln1_g[l], ln1_b[l])
        mix = hybrid_mixer(x, w_in[l], conv_w[l], conv_b[l], rg_w_a[l], rg_b_a[l], rg_w_x[l], rg_b_x[l],
                           rg_lambda[l], fox_b_f[l],
                           s5_a_re[l], s5_a_im[l], s5_log_dt[l], s5_b_re[l], s5_b_im[l],
                           s5_c_re[l], s5_c_im[l], s5_d[l], s5_w_glu[l],
                           mix_norm_g[l], w_out[l])
        x = layer_norm(ALPHA * x + mix, ln2_g[l], ln2_b[l])
        x = layer_norm(ALPHA * x + 0.5 * swiglu(x, ffn2_w_gate[l], ffn2_w_up[l], ffn2_w_down[l]),
                       ln3_g[l], ln3_b[l])
    return x


_drawn_inputs = setup_inputs


def setup_inputs(seed=0):
    import zlib

    import numpy as np

    out = dict(_drawn_inputs(seed))
    spreads = {}
    factors = {'rg_b_a': 8.0,
     'rg_b_x': 8.0,
     'fox_b_f': 34.304,
     's5_a_re': 64.0,
     's5_a_im': 31.384,
     's5_log_dt': 32.416,
     's5_b_re': 44.44,
     's5_b_im': 43.672,
     's5_c_re': 45.376,
     's5_c_im': 45.264,
     'mix_norm_g': 5.567}
    for name, (base, spread) in spreads.items():
        noise = np.random.default_rng([zlib.crc32(name.encode()), seed]).standard_normal(out[name].shape)
        drawn = base * np.exp(spread * noise) if base else spread * noise
        out[name] = __import__('jax').numpy.asarray(drawn.astype(out[name].dtype))
    for name, factor in factors.items():
        out[name] = (out[name] * factor).astype(out[name].dtype)
    return out
```

```python
from contextlib import ExitStack
import math

import concourse.bass as bass
from concourse import mybir

ALU = mybir.AluOpType
ACT = mybir.ActivationFunctionType
F32 = mybir.dt.float32
F32R = mybir.dt.float32r
I32 = mybir.dt.int32

P = 128
DEPTH, SEQ, DM, DFF = 2, 256, 1024, 2816
KD = DM // P
TT = SEQ // P
DA = DB = 384
DC = 256
HEADS, HD = 6, 64
CGROUP, CSTATE = 16, 64
S5_TILES = (DC // CGROUP) * CSTATE // P
NIN = 2 * DA + 3 * DB + HEADS + DC
ALPHA = (2 * DEPTH) ** 0.25
LN_EPS, RMS_EPS, RG_C = 1e-5, 1e-6, 8.0

PC = 256
PAIRS = DFF // PC
RING = 3
FFN_N = 3 * PAIRS
MIX_N = 13
LAYER_N = 2 * FFN_N + MIX_N
FFN_BASE = (0, FFN_N + MIX_N)
MIX_BASE = FFN_N
LEAD = 2
SLOT_USES = [len(range(s, LAYER_N, RING)) for s in range(RING)]
CREDIT = 3
HALVES = (PAIRS - 1) // 2

ZPIECES = [(NIN - DC, PC), (0, PC), (PC, PC), (2 * PC, PC), (4 * DA + PC, DB - PC + HEADS), (4 * DA, PC),
           (3 * PC, PC), (4 * PC, PC), (5 * PC, PC)]
WOUT_ROWS = [3 * PC, 0, PC, 2 * PC]
VT_W = DB - PC + HEADS

ROW = {}
_at = 0
for _name, _n in (("a_re", 8), ("a_im", 8), ("ln1_g", 8), ("ln1_b", 8), ("ln2_g", 8), ("ln2_b", 8),
                  ("ln3_g", 8), ("ln3_b", 8), ("conv_w", 12), ("conv_b", 3), ("b_a", 3), ("b_x", 3),
                  ("lam", 3), ("mix_g", 8), ("log_dt", 8), ("d", 2)):
    ROW[_name] = _at
    _at += _n
NPAR = _at

N_PARAM_DMAS = 26
PAR_V_ANGLE = 11
PAR_V_DONE = 47
TAB_MATS = 12
TAB_DONE = TAB_MATS + 2 + 11 * 8
RG_V_OM = 2
RG_V_DONE = 8
F_V_DONE = 17
XTOK_SCALED = (2, 8, 14)
XTOK_AFFINE = (6, 12, 18)


def trunk(nc, x, w, out):
    ctx = ExitStack()
    with ctx:
        ctx.enter_context(nc.allow_non_contiguous_dma(reason="small parameters"))

        def sb(name, shape, dt=F32):
            return ctx.enter_context(nc.sbuf_tensor(name, shape, dt))

        def ps(name):
            return ctx.enter_context(nc.psum_tensor(name, [P, 512], F32))

        raw = sb("raw", [P, RING, 8 * PC])
        whi = sb("whi", [P, RING, 8 * PC], F32R)
        wlo = sb("wlo", [P, RING, 8 * PC], F32R)
        xT_hi = sb("xT_hi", [P, KD, SEQ], F32R)
        xT_lo = sb("xT_lo", [P, KD, SEQ], F32R)
        xT_f = sb("xT_f", [P, 2, 4, P])
        xtok = sb("xtok", [P, TT, DM])
        xn = sb("xn", [P, TT, DM])
        lngb = sb("lngb", [P, 2, DM])
        act_hi = sb("act_hi", [P, 4, SEQ], F32R)
        act_lo = sb("act_lo", [P, 4, SEQ], F32R)
        bn = sb("bn", [P, TT, 2, 6])
        mv = sb("mv", [P, TT, 2])
        std = sb("std", [P, TT])
        rstd = sb("rstd", [P, TT])
        ident = sb("ident", [P, P])
        mask = sb("mask", [P, SEQ])
        tri = sb("tri", [P, SEQ])
        ones = sb("ones", [P, 2])
        eps = sb("eps", [P, 2])
        gidx = sb("gidx", [P, 1], I32)
        gbit = sb("gbit", [P, 1], I32)
        oddg = sb("oddg", [P, 2])
        parR = sb("parR", [P, P])
        par = sb("par", [P, P])
        dtrow = sb("dtrow", [P, 2])
        ec = sb("ec", [P, S5_TILES, SEQ])
        es = sb("es", [P, S5_TILES, SEQ])
        pq = sb("pq", [P, 24, 8])
        rg = sb("rg", [P, 16, 3])
        wp = sb("wp", [P, 5, 8])
        bnat = sb("bnat", [P, 2, 8, CGROUP])
        cnat = sb("cnat", [P, 2, 2, CSTATE])
        bexp = sb("bexp", [P, 2, 8, 2 * CGROUP])
        cexp = sb("cexp", [P, 2, 2, 2, CSTATE])
        bT = sb("bT", [P, 4, P])
        cT = sb("cT", [P, 4, P])
        wrg = sb("wrg", [P, 2, 3, P])
        wglu = sb("wglu", [P, 2, DC])
        bf = sb("bf", [P, HEADS])
        ax = sb("ax", [P, 3, SEQ + 3])
        gg = sb("gg", [P, 3, SEQ])
        qT = sb("qT", [P, 3, SEQ])
        kT = sb("kT", [P, 3, SEQ])
        vv = sb("vv", [P, TT, DB])
        uT = sb("uT", [P, 2, SEQ])
        xa = sb("xa", [P, 3, SEQ])
        ig = sb("ig", [P, 3, SEQ])
        av = sb("av", [P, 3, SEQ])
        th = sb("th", [P, 3, SEQ])
        gin = sb("gin", [P, 2, 2, SEQ])
        gs = sb("gs", [P, 2, SEQ])
        hh = sb("hh", [P, 2, 2, SEQ])
        osq = sb("osq", [P, 3, SEQ])
        flog = sb("flog", [P, TT, HEADS])
        fx = sb("fx", [P, 8, TT, HEADS])
        logf = sb("logf", [P, TT, HEADS])
        crow = sb("crow", [P, 2, SEQ])
        mx = sb("mx", [P, HEADS, 2])
        nmx = sb("nmx", [P, HEADS, 2])
        rsum = sb("rsum", [P, HEADS, 2])
        rrec = sb("rrec", [P, HEADS, 2])
        gstd = sb("gstd", [P, 3, TT])
        grstd = sb("grstd", [P, 3, TT])

        silu = kT[:, 0:2, :].rearrange("p a n -> p (a n)")
        hid = qT[:, 0:2, :].rearrange("p a n -> p (a n)")
        btmp = xa[:, 0:2, :].rearrange("p a (b c) -> p (a b) c", c=CGROUP).rearrange("p (a b) c -> p a b c", a=4)
        s5_t = xn[:, 0, :].rearrange("p (a n) -> p a n", a=4)
        s5_m = xn[:, 1, :].rearrange("p (a n) -> p a n", a=4)
        prob = [xn[:, 0, i * 384:(i + 1) * 384] for i in range(2)]
        probT = [xn[:, 1, i * 384:(i + 1) * 384] for i in range(2)]
        cA, cB = ec[0:2, 0:HEADS, :], es[0:2, 0:HEADS, :]

        bank = [ps(f"bank{i}") for i in range(8)]

        def sem(name):
            return ctx.enter_context(nc.semaphore(name))

        x_loaded = sem("x_loaded")
        const_pool = sem("const_pool")
        const_vec = sem("const_vec")
        raw_loaded = [sem(f"raw_loaded{s}") for s in range(RING)]
        hi_done = sem("hi_done")
        lo_done = sem("lo_done")
        pieces_used = sem("pieces_used")
        lngb_loaded = sem("lngb_loaded")
        layer_arrived = sem("layer_arrived")
        loads_begun = sem("loads_begun")
        layer_closed = sem("layer_closed")
        layer_open = sem("layer_open")
        x0_transposed = sem("x0_transposed")
        x0_hi = sem("x0_hi")
        x0_lo = sem("x0_lo")
        stored = sem("stored")

        local = []

        def lsem(name):
            s = sem(name)
            local.append(s)
            return s

        params_loaded = lsem("params_loaded")
        dt_spread = lsem("dt_spread")
        par_turned = lsem("par_turned")
        par_ready = lsem("par_ready")
        par_v = lsem("par_v")
        par_a = lsem("par_a")
        tab_step = lsem("tab_step")
        bc_turned = lsem("bc_turned")
        bc_ready = lsem("bc_ready")
        silu_done = lsem("silu_done")
        hid_done = lsem("hid_done")
        hid_hi = lsem("hid_hi")
        hid_lo = lsem("hid_lo")
        y0_ready = lsem("y0_ready")
        ln_v = lsem("ln_v")
        mv_ready = lsem("mv_ready")
        std_ready = lsem("std_ready")
        xn_ready = lsem("xn_ready")
        xT_turned = lsem("xT_turned")
        xT_affine = lsem("xT_affine")
        xT_hi_done = lsem("xT_hi_done")
        xT_lo_done = lsem("xT_lo_done")
        xtok_step = lsem("xtok_step")
        z_half = lsem("z_half")
        z_evac = lsem("z_evac")
        f_evac = lsem("f_evac")
        conv_step = lsem("conv_step")
        gates_ready = lsem("gates_ready")
        gate_sig = lsem("gate_sig")
        decay_done = lsem("decay_done")
        rg_v = lsem("rg_v")
        sqrt_done = lsem("sqrt_done")
        bu_ready = lsem("bu_ready")
        bu_mul = lsem("bu_mul")
        gin_done = lsem("gin_done")
        s5_scan = lsem("s5_scan")
        s5_rot = lsem("s5_rot")
        h_done = lsem("h_done")
        y_done = lsem("y_done")
        ys_step = lsem("ys_step")
        ys_gelu = lsem("ys_gelu")
        glu_ready = lsem("glu_ready")
        glu_sig = lsem("glu_sig")
        oc_done = lsem("oc_done")
        f_v = lsem("f_v")
        f_a = lsem("f_a")
        c_ready = lsem("c_ready")
        c_evac = lsem("c_evac")
        c_ones = lsem("c_ones")
        c_loaded = lsem("c_loaded")
        s_ready = lsem("s_ready")
        l_done = lsem("l_done")
        nmx_done = lsem("nmx_done")
        p_done = lsem("p_done")
        pn_step = lsem("pn_step")
        pt_ready = lsem("pt_ready")
        pt_evac = lsem("pt_evac")
        pv_done = lsem("pv_done")
        ob_evac = lsem("ob_evac")
        o_hi = lsem("o_hi")
        o_lo = lsem("o_lo")
        o_sq = lsem("o_sq")
        ss_ready = lsem("ss_ready")
        gstd_done = lsem("gstd_done")
        grstd_done = lsem("grstd_done")
        proj_ready = lsem("proj_ready")
        proj_evac = lsem("proj_evac")
        nums = [s.num for s in local]
        assert nums == list(range(nums[0], nums[0] + len(nums))), nums
        local_range = range(nums[0], nums[0] + len(nums))

        def used(L, pos):
            return L * LAYER_N + pos + 1 + CREDIT

        def slot_before(L, pos0, step):
            if isinstance(step, int) and pos0 + step < RING:
                last = max(q for q in range(LAYER_N) if q % RING == (pos0 + step) % RING)
                return used(L, last - LAYER_N)
            return used(L, step + (pos0 - RING))

        def loaded(L, pos0, step, turns):
            return (L * SLOT_USES[pos0 % RING] + turns + (pos0 // RING + 1)) * 16

        gate_w = [w[f"ffn{f}_w_gate"].rearrange("l (k p) (j n) -> l j p k n", p=P, n=PC) for f in (1, 2)]
        up_w = [w[f"ffn{f}_w_up"].rearrange("l (k p) (j n) -> l j p k n", p=P, n=PC) for f in (1, 2)]
        down_w = [w[f"ffn{f}_w_down"].rearrange("l (j k p) n -> l j p k n", p=P, k=2) for f in (1, 2)]
        win = w["w_in"].rearrange("l (k p) n -> l p k n", p=P)
        wout = w["w_out"].rearrange("l (k p) n -> l p k n", p=P)

        def pair_pos(f, q):
            b = FFN_BASE[f] + 2 + 3 * q
            return b, b + 1, b + 2

        def piece(t, pos, k, n):
            return t[:, pos % RING, 0:k * n].rearrange("p (k n) -> p k n", n=n)

        def width(pos):
            m = pos - MIX_BASE
            return 8 * VT_W if m == 4 else 8 * PC

        def prow(name, n):
            return par[:, ROW[name] + n:ROW[name] + n + 1]

        FFN_LN = (0, 2)
        LN_NAMES = ("ln1", "ln2", "ln3")
        V_EVENTS = (8, 9, 10, 11)

        block = ctx.enter_context(nc.Block())

        @block.sync
        def _(sp):
            sp.dma_start(xtok[:, :, :], x[0].rearrange("(t p) n -> p t n", p=P)).then_inc(x_loaded, 16)

            def load(L, pos0, step, turns, src, k, n):
                sp.wait_ge(lo_done, slot_before(L, pos0, step))
                sp.sem_inc(loads_begun, 1)
                sp.dma_start(piece(raw, pos0, k, n), src).then_inc(raw_loaded[pos0 % RING], 16)

            def ffn(L, f):
                b = FFN_BASE[f]
                load(L, b, 0, 0, gate_w[f][L, 0], 8, PC)
                load(L, b + 1, 0, 0, up_w[f][L, 0], 8, PC)
                with sp.Fori(0, HALVES) as i:
                    for q in (0, 1):
                        g, u, d = pair_pos(f, q)
                        load(L, g, i * 6, i * 2, gate_w[f][L, i * 2 + (q + 1)], 8, PC)
                        load(L, u, i * 6, i * 2, up_w[f][L, i * 2 + (q + 1)], 8, PC)
                        load(L, d, i * 6, i * 2, down_w[f][L, i * 2 + q], 2, DM)
                load(L, b + FFN_N - 1, 0, 0, down_w[f][L, PAIRS - 1], 2, DM)

            with sp.Fori(0, DEPTH) as L:
                ffn(L, 0)
                for m, (col, n) in enumerate(ZPIECES):
                    load(L, MIX_BASE + m, 0, 0, win[L, :, :, col:col + n], 8, n)
                for m, row in enumerate(WOUT_ROWS):
                    load(L, MIX_BASE + len(ZPIECES) + m, 0, 0, wout[L, :, row // P:row // P + 2, :], 2, DM)
                ffn(L, 1)
            sp.wait_ge(layer_arrived, 4 * DEPTH + 1)
            sp.dma_start(out[0].rearrange("(t p) n -> p t n", p=P), xtok[:, :, :]).then_inc(stored, 16)
            sp.wait_ge(stored, 16)

        @block.gpsimd
        def _(pool):
            pool.memset(ident[:, :], 0.0).then_inc(const_pool, 1)
            pool.memset(mask[:, :], 0.0).then_inc(const_pool, 1)
            pool.memset(tri[:, :], 1.0).then_inc(const_pool, 1)
            pool.memset(ones[:, :], 1.0).then_inc(const_pool, 1)
            pool.memset(eps[:, 0:1], LN_EPS).then_inc(const_pool, 1)
            pool.memset(eps[:, 1:2], RMS_EPS).then_inc(const_pool, 1)
            pool.memset(ax[:, :, 0:3], 0.0).then_inc(const_pool, 1)
            pool.memset(parR[:, :], 0.0).then_inc(const_pool, 1)
            pool.memset(wrg[:, :, :, :], 0.0).then_inc(const_pool, 1)
            pool.memset(bexp[:, :, :, :], 0.0).then_inc(const_pool, 1)
            pool.iota(gidx[:, :], [[0, 1]], base=0, channel_multiplier=1).then_inc(const_pool, 1)
            pool.wait_ge(const_pool, 11)
            pool.affine_select(out=ident[:, :], in_=ident[:, :], compare_op=ALU.not_equal, fill=1.0, base=0,
                               pattern=[[-1, P]], channel_multiplier=1).then_inc(const_pool, 1)
            pool.affine_select(out=mask[:, P:], in_=mask[:, P:], compare_op=ALU.is_ge, fill=-1e30, base=0,
                               pattern=[[-1, P]], channel_multiplier=1).then_inc(const_pool, 1)
            pool.affine_select(out=tri[:, :], in_=tri[:, :], compare_op=ALU.is_ge, fill=0.0, base=0,
                               pattern=[[1, SEQ]], channel_multiplier=-1).then_inc(const_pool, 1)

            with pool.Fori(0, DEPTH) as L:
                steps = [0]

                def mark_x(ins):
                    steps[0] += 1
                    ins.then_inc(xtok_step, 1)

                def load_gb(n):
                    for h, k in enumerate("gb"):
                        src = w[f"{LN_NAMES[n]}_{k}"][L]
                        src = src.rearrange("(o n) -> o n", o=1).to_broadcast([P, DM])
                        pool.dma_start(lngb[:, h, :], src).then_inc(lngb_loaded, 16)

                def scale_residual():
                    if steps[0]:
                        pool.wait_ge(xtok_step, steps[0])
                    for t in range(TT):
                        mark_x(pool.tensor_scalar(xtok[:, t, :], xtok[:, t, :], ALPHA, 1.0, ALU.mult, ALU.mult))

                def affine(n):
                    pool.wait_ge(lngb_loaded, L * 96 + 32 * (n + 1))
                    for t in range(TT):
                        pool.wait_ge(xn_ready, TT * n + t + 1)
                        mark_x(pool.tensor_tensor(xtok[:, t, :], xn[:, t, :], lngb[:, 0, :], ALU.mult))
                        pool.wait_ge(xtok_step, steps[0])
                        mark_x(pool.tensor_tensor(xtok[:, t, :], xtok[:, t, :], lngb[:, 1, :], ALU.add))
                    pool.wait_ge(xtok_step, steps[0])

                pool.wait_ge(x_loaded, 16)
                pool.wait_ge(x0_transposed, 4)
                scale_residual()
                load_gb(0)

                tabs = [0]

                def tab(ins, settle=True):
                    tabs[0] += 1
                    ins.then_inc(tab_step, 1)
                    if settle:
                        pool.wait_ge(tab_step, tabs[0])

                pool.wait_ge(const_vec, 3)
                pool.wait_ge(params_loaded, 16 * N_PARAM_DMAS)
                for r in range(2):
                    for half in range(2):
                        tab(pool.tensor_scalar(cexp[:, :, r, half, :], cnat[:, r, :, :], oddg[:, half:half + 1],
                                               1.0 if r == 0 else -1.0, ALU.mult, ALU.mult), settle=False)
                pool.wait_ge(par_v, PAR_V_DONE)
                cr = pq[:, 20, :].rearrange("p (a o) -> p a o", o=1).to_broadcast([P, 8, CGROUP])
                ci = pq[:, 21, :].rearrange("p (a o) -> p a o", o=1).to_broadcast([P, 8, CGROUP])
                tab(pool.tensor_tensor(btmp[:, 0], bnat[:, 0], cr, ALU.mult), settle=False)
                tab(pool.tensor_tensor(btmp[:, 1], bnat[:, 1], ci, ALU.mult), settle=False)
                tab(pool.tensor_tensor(btmp[:, 2], bnat[:, 1], cr, ALU.mult), settle=False)
                tab(pool.tensor_tensor(btmp[:, 3], bnat[:, 0], ci, ALU.mult))
                for half in range(2):
                    rows = slice(64 * half, 64 * half + 64)
                    cols = slice(CGROUP * half, CGROUP * half + CGROUP)
                    tab(pool.tensor_tensor(bexp[rows, 0, :, cols], btmp[rows, 0], btmp[rows, 1], ALU.subtract))
                    tab(pool.tensor_tensor(bexp[rows, 1, :, cols], btmp[rows, 2], btmp[rows, 3], ALU.add))
                tab(pool.memset(ec[:, :, 0:1], 1.0), settle=False)
                tab(pool.memset(es[:, :, 0:1], 0.0))
                cw, sw = pq[:, 10, :], pq[:, 11, :]
                n = 1
                while n < SEQ:
                    cb = cw.rearrange("p (a o) -> p a o", o=1).to_broadcast([P, 8, n])
                    sbr = sw.rearrange("p (a o) -> p a o", o=1).to_broadcast([P, 8, n])
                    tab(pool.tensor_tensor(ec[:, :, n:2 * n], ec[:, :, 0:n], cb, ALU.mult), settle=False)
                    tab(pool.tensor_tensor(es[:, :, n:2 * n], es[:, :, 0:n], cb, ALU.mult), settle=False)
                    t0 = xn[:, 0, :].rearrange("p (a n) -> p a n", a=S5_TILES)[:, :, 0:n]
                    t1 = xn[:, 1, :].rearrange("p (a n) -> p a n", a=S5_TILES)[:, :, 0:n]
                    tab(pool.tensor_tensor(t0, es[:, :, 0:n], sbr, ALU.mult), settle=False)
                    tab(pool.tensor_tensor(t1, ec[:, :, 0:n], sbr, ALU.mult))
                    tab(pool.tensor_tensor(ec[:, :, n:2 * n], ec[:, :, n:2 * n], t0, ALU.subtract), settle=False)
                    tab(pool.tensor_tensor(es[:, :, n:2 * n], es[:, :, n:2 * n], t1, ALU.add), settle=False)
                    tab(pool.tensor_tensor(wp[:, 2, :], cw, cw, ALU.mult), settle=False)
                    tab(pool.tensor_tensor(wp[:, 3, :], sw, sw, ALU.mult), settle=False)
                    tab(pool.tensor_tensor(wp[:, 4, :], cw, sw, ALU.mult))
                    tab(pool.tensor_tensor(wp[:, 0, :], wp[:, 2, :], wp[:, 3, :], ALU.subtract), settle=False)
                    tab(pool.tensor_tensor(wp[:, 1, :], wp[:, 4, :], wp[:, 4, :], ALU.add))
                    cw, sw = wp[:, 0, :], wp[:, 1, :]
                    n *= 2
                assert tabs[0] == TAB_DONE, tabs

                affine(0)
                scale_residual()
                load_gb(1)

                for i in range(S5_TILES):
                    pool.wait_ge(bu_mul, 2 * i + 2)
                    if i >= 2:
                        pool.wait_ge(s5_scan, 2 * i - 2)
                    pool.tensor_tensor(gin[:, i % 2, 0, :], s5_t[:, 0, :], s5_t[:, 3, :], ALU.add).then_inc(gin_done, 1)
                    pool.tensor_tensor(gin[:, i % 2, 1, :], s5_t[:, 1, :], s5_t[:, 2, :], ALU.subtract)\
                        .then_inc(gin_done, 1)
                    pool.wait_ge(s5_rot, 2 * i + 2)
                    if i >= 2:
                        pool.wait_ge(y_done, i - 1)
                    pool.tensor_tensor(hh[:, i % 2, 0, :], s5_m[:, 0, :], s5_m[:, 3, :], ALU.subtract)\
                        .then_inc(h_done, 1)
                    pool.tensor_tensor(hh[:, i % 2, 1, :], s5_m[:, 1, :], s5_m[:, 2, :], ALU.add).then_inc(h_done, 1)
                pool.memset(cA, 1.0).then_inc(c_ones, 1)
                pool.memset(cB, 1.0).then_inc(c_ones, 1)

                def squares(g, src, n, first):
                    if first:
                        pool.wait_ge(ss_ready, first)
                    for t in range(n):
                        if g == 2:
                            pool.wait_ge(ob_evac, t + 1)
                        pool.tensor_tensor(osq[:, t, :], src[:, t, :], src[:, t, :], ALU.mult).then_inc(o_sq, 1)

                pool.wait_ge(oc_done, 2)
                squares(0, uT, 2, 0)
                pool.wait_ge(rg_v, RG_V_DONE)
                squares(1, gg, 3, 1)
                squares(2, qT, 3, 2)

                affine(1)
                scale_residual()
                load_gb(2)
                affine(2)
                pool.drain().then_inc(layer_arrived, 1)
                pool.wait_ge(layer_arrived, L * 4 + 4)
                pool.sem_inc(layer_closed, 1)
                pool.sem_clear(local_range)
                pool.sem_inc(layer_open, 1)
            pool.sem_inc(layer_arrived, 1)

        @block.scalar
        def _(act):
            A = nc.scalar

            def split_hi(L, pos0, step, turns, n):
                act.wait_ge(raw_loaded[pos0 % RING], loaded(L, pos0, step, turns))
                act.wait_ge(pieces_used, slot_before(L, pos0, step))
                A.activation(whi[:, pos0 % RING, 0:n], raw[:, pos0 % RING, 0:n], ACT.Copy).then_inc(hi_done, 1)

            act.sem_inc(hi_done, CREDIT)
            for e in range(4):
                act.wait_ge(x0_transposed, e + 1)
                A.activation(xT_hi[:, 4 * (e % 2):4 * (e % 2) + 4, (e // 2) * P:(e // 2 + 1) * P],
                             bank[4 + e][:, :].rearrange("p (a n) -> p a n", a=4), ACT.Copy).then_inc(x0_hi, 1)

            with act.Fori(0, DEPTH) as L:
                def prologue_splits(f):
                    for r in range(LEAD):
                        split_hi(L, FFN_BASE[f] + r, 0, 0, 8 * PC)

                def ffn_pair(L, f, j, q, i):
                    last = isinstance(i, int)
                    g, u, d = pair_pos(f, q)
                    i6, i2 = i * 6, i * 2

                    def ahead(pos):
                        rel = pos + LEAD - FFN_BASE[f] + (6 * i if last else 0)
                        if rel >= FFN_N and f == 1:
                            return
                        split_hi(L, pos + LEAD, i6, i2, 8 * PC)
                    ahead(g)
                    act.wait_ge(pieces_used, used(L, i6 + g))
                    act.wait_ge(hid_done, i2 + (PAIRS * f + q + 1))
                    A.activation(silu, bank[4 + (q + 1) % 2][:, :], ACT.Silu).then_inc(silu_done, 1)
                    ahead(u)
                    act.wait_ge(hid_done, i2 + (PAIRS * f + q + 2))
                    act.wait_ge(pieces_used, used(L, i6 + (d - 3)))
                    o = 2 * ((q + 1) % 2)
                    A.activation(act_hi[:, o:o + 2, :], hid.rearrange("p (a n) -> p a n", a=2), ACT.Copy)\
                        .then_inc(hid_hi, 1)
                    ahead(d)

                def ffn(f):
                    b = FFN_BASE[f]
                    split_hi(L, b + LEAD, 0, 0, 8 * PC)
                    act.wait_ge(pieces_used, used(L, b))
                    if f:
                        act.wait_ge(hid_done, PAIRS)
                    A.activation(silu, bank[4][:, :], ACT.Silu).then_inc(silu_done, 1)
                    split_hi(L, b + 1 + LEAD, 0, 0, 8 * PC)
                    act.wait_ge(hid_done, PAIRS * f + 1)
                    A.activation(act_hi[:, 0:2, :], hid.rearrange("p (a n) -> p a n", a=2), ACT.Copy)\
                        .then_inc(hid_hi, 1)
                    if f == 0:
                        param_functions()
                    with act.Fori(0, HALVES - 1) as i:
                        for q in (0, 1):
                            ffn_pair(L, f, None, q, i)
                    for q in (0, 1):
                        ffn_pair(L, f, None, q, HALVES - 1)
                    if f == 0:
                        split_hi(L, b + FFN_N - 1 + LEAD, 0, 0, 8 * PC)

                def param_functions():
                    def f(need, out, in_, fn, **kw):
                        act.wait_ge(par_v, need)
                        A.activation(out, in_, fn, **kw).then_inc(par_a, 1)
                    act.wait_ge(par_ready, 1)
                    A.activation(pq[:, 0, :], par[:, ROW["log_dt"]:ROW["log_dt"] + 8], ACT.Exp).then_inc(par_a, 1)
                    A.activation(rg[:, 0, :], par[:, ROW["lam"]:ROW["lam"] + 3], ACT.Abs).then_inc(par_a, 1)
                    act.wait_ge(par_a, 2)
                    A.activation(rg[:, 1, :], rg[:, 0, :], ACT.Exp, scale=-1.0).then_inc(par_a, 1)
                    f(1, pq[:, 3, :], pq[:, 1, :], ACT.Exp)
                    f(1, pq[:, 4, :], pq[:, 1, :], ACT.Tanh, scale=0.5)
                    f(PAR_V_ANGLE, pq[:, 8, :], pq[:, 6, :], ACT.Sin)
                    f(PAR_V_ANGLE, pq[:, 9, :], pq[:, 7, :], ACT.Sin)

                def layer_norm(n):
                    for t in range(TT):
                        act.wait_ge(mv_ready, TT * n + t + 1)
                        A.activation(std[:, t:t + 1], mv[:, t, 1:2], ACT.Sqrt, bias=eps[:, 0:1]).then_inc(std_ready, 1)
                    g0, b0 = LN_NAMES[n] + "_g", LN_NAMES[n] + "_b"
                    for t in range(TT):
                        for b in range(2):
                            e = 4 * n + 2 * t + b
                            act.wait_ge(xT_turned, e + 1)
                            if e >= 2:
                                act.wait_ge(xT_lo_done, e - 1)
                            for k in range(4):
                                ins = A.activation(xT_f[:, b, k, :], bank[4 + 2 * t + b][:, k * P:(k + 1) * P],
                                                   ACT.Identity, bias=prow(b0, 4 * b + k), scale=prow(g0, 4 * b + k))
                            ins.then_inc(xT_affine, 1)

                def pload(dst, src):
                    act.dma_start(dst, src).then_inc(params_loaded, 16)

                act.wait_ge(const_pool, 14)
                rows = {"a_re": "s5_a_re", "a_im": "s5_a_im", "ln1_g": "ln1_g", "ln1_b": "ln1_b", "ln2_g": "ln2_g",
                        "ln2_b": "ln2_b", "ln3_g": "ln3_g", "ln3_b": "ln3_b", "conv_w": "conv_w",
                        "conv_b": "conv_b", "b_a": "rg_b_a", "b_x": "rg_b_x", "lam": "rg_lambda",
                        "mix_g": "mix_norm_g", "d": "s5_d"}
                for name, key in rows.items():
                    src = w[key]
                    if name == "conv_w":
                        src = src.rearrange("l k (t n) -> l (k t) n", n=P)
                    elif key in ("s5_a_re", "s5_a_im"):
                        src = src.rearrange("l (r g) s -> l r (g s)", g=2)
                    else:
                        src = src.rearrange("l (r n) -> l r n", n=P)
                    pload(parR[ROW[name]:ROW[name] + src.shape[1], :], src[L])
                pload(dtrow[96:104, :], w["s5_log_dt"].rearrange("l (t g) -> l t g", g=2)[L])
                for r, c in enumerate(("re", "im")):
                    pload(bnat[:, r, :, :],
                          w[f"s5_b_{c}"].rearrange("l (t g) s c -> l (g s) t c", g=2)[L])
                    pload(cnat[:, r, :, :],
                          w[f"s5_c_{c}"].rearrange("l (q g) c s -> l (g c) q s", q=2)[L])
                for a, key in enumerate(("rg_w_a", "rg_w_x")):
                    for h in range(2):
                        pload(wrg[64 * h:64 * h + 64, a, :, 64 * h:64 * h + 64],
                              w[key].rearrange("l (t h) i o -> l h i t o", h=2)[L, h])
                pload(wglu[:, :, :], w["s5_w_glu"].rearrange("l (k p) n -> l p k n", p=P)[L])
                pload(bf[:, :], w["fox_b_f"][L].rearrange("(o n) -> o n", o=1).to_broadcast([P, HEADS]))
                assert len(rows) + 11 == N_PARAM_DMAS

                prologue_splits(0)
                ffn(0)
                for r, dst in ((7, bT), (6, cT)):
                    act.wait_ge(bc_turned, 1 if r == 7 else 2)
                    A.activation(dst[:, :, :].rearrange("p a n -> p (a n)"), bank[r][:, :], ACT.Copy)\
                        .then_inc(bc_ready, 1)
                layer_norm(0)

                def ahead(m):
                    pos = MIX_BASE + m + LEAD
                    if m + LEAD < MIX_N:
                        split_hi(L, pos, 0, 0, width(pos))

                def z_wait(e):
                    if e % 2 == 0:
                        act.wait_ge(z_half, e // 2 + 1)
                    else:
                        act.wait_ge(pieces_used, used(L, MIX_BASE + e // 2))

                def evac(e, dst, fn=ACT.Copy, **kw):
                    z_wait(e)
                    A.activation(dst, bank[e % 4][:, 0:SEQ], fn, **kw).then_inc(z_evac, 1)

                ahead(0)
                evac(0, uT[:, 0, :])
                evac(1, uT[:, 1, :])
                ahead(1)
                evac(2, ax[:, 0, 3:])
                evac(3, ax[:, 1, 3:])
                ahead(2)
                evac(4, ax[:, 2, 3:])
                evac(5, gg[:, 0, :], ACT.Gelu_apprx_tanh)
                ahead(3)
                evac(6, gg[:, 1, :], ACT.Gelu_apprx_tanh)
                evac(7, gg[:, 2, :], ACT.Gelu_apprx_tanh)
                ahead(4)

                def gate_sigmoids(f):
                    act.wait_ge(gates_ready, f + 1)
                    A.activation(av[:, f, :], bank[4][:, 0:SEQ], ACT.Sigmoid, bias=prow("b_a", f)).then_inc(gate_sig, 1)
                    A.activation(ig[:, f, :], bank[4][:, SEQ:], ACT.Sigmoid, bias=prow("b_x", f)).then_inc(gate_sig, 1)

                gate_sigmoids(0)
                gate_sigmoids(1)
                for t in range(TT):
                    z_wait(8 + t)
                    A.activation(flog[:, t, :], bank[t][:, DB - PC:VT_W], ACT.Copy).then_inc(f_evac, 1)
                    A.activation(vv[:, t, PC:], bank[t][:, 0:DB - PC], ACT.Copy).then_inc(z_evac, 1)
                ahead(5)
                gate_sigmoids(2)
                act.wait_ge(gate_sig, 6)
                for f in range(3):
                    A.activation(th[:, f, :], av[:, f, :], ACT.Tanh, scale=rg[:, 13, f:f + 1]).then_inc(decay_done, 1)
                    act.wait_ge(decay_done, 2 * f + 1)
                    A.activation(av[:, f, :], av[:, f, :], ACT.Exp, scale=rg[:, 14, f:f + 1]).then_inc(decay_done, 1)
                act.wait_ge(f_v, 1)
                A.activation(fx[:, 1], fx[:, 0], ACT.Abs).then_inc(f_a, 1)
                act.wait_ge(f_a, 1)
                A.activation(fx[:, 2], fx[:, 1], ACT.Exp, scale=-1.0).then_inc(f_a, 1)
                for t in range(TT):
                    z_wait(10 + t)
                    A.activation(vv[:, t, 0:PC], bank[2 + t][:, 0:PC], ACT.Copy).then_inc(z_evac, 1)
                ahead(6)
                act.wait_ge(rg_v, RG_V_OM)
                A.activation(th[:, :, :], th[:, :, :], ACT.Sqrt).then_inc(sqrt_done, 1)
                evac(12, qT[:, 0, :], scale=HD ** -0.5)
                evac(13, qT[:, 1, :], scale=HD ** -0.5)
                ahead(7)
                evac(14, qT[:, 2, :], scale=HD ** -0.5)
                evac(15, kT[:, 0, :])
                ahead(8)
                evac(16, kT[:, 1, :])
                evac(17, kT[:, 2, :])
                act.wait_ge(c_ready, 1)
                A.activation(crow[0:HEADS, 0, :], bank[4][0:HEADS, 0:SEQ], ACT.Copy).then_inc(c_evac, 1)
                A.activation(crow[0:HEADS, 1, :], bank[4][0:HEADS, 0:SEQ], ACT.Copy, scale=-1.0).then_inc(c_evac, 1)
                act.wait_ge(c_evac, 2)
                act.wait_ge(c_ones, 2)
                act.dma_start(ec[0:1, 0:HEADS, :], crow[0:HEADS, 0, :]).then_inc(c_loaded, 16)
                act.dma_start(es[1:2, 0:HEADS, :], crow[0:HEADS, 1, :]).then_inc(c_loaded, 16)
                act.wait_ge(ys_step, 2)
                A.activation(gs[:, :, :], gs[:, :, :], ACT.Gelu_apprx_tanh).then_inc(ys_gelu, 1)
                act.wait_ge(glu_ready, 1)
                A.activation(gin[:, 0, :, :], bank[2][:, :].rearrange("p (a n) -> p a n", a=2), ACT.Sigmoid)\
                    .then_inc(glu_sig, 1)

                def out_hi(tile, src, first_used):
                    if tile >= 4:
                        act.wait_ge(pieces_used, used(L, MIX_BASE + first_used))
                    g = {0: 6, 1: 7}.get(tile, tile - 2)
                    A.activation(act_hi[:, tile % 4, :], src, ACT.Copy, scale=prow("mix_g", g)).then_inc(o_hi, 1)

                def group_std(g, n):
                    act.wait_ge(ss_ready, g + 1)
                    A.activation(gstd[:, g, :], bank[4][:, 384:386], ACT.Sqrt, bias=eps[:, 1:2], scale=1.0 / n)\
                        .then_inc(gstd_done, 1)

                act.wait_ge(oc_done, 2)
                out_hi(0, uT[:, 0, :], 0)
                out_hi(1, uT[:, 1, :], 0)
                act.wait_ge(rg_v, RG_V_DONE)
                out_hi(2, gg[:, 0, :], 0)
                out_hi(3, gg[:, 1, :], 0)
                group_std(0, DC)
                ahead(9)
                out_hi(4, gg[:, 2, :], 9)
                group_std(1, DA)
                ahead(10)

                def attn_exp(h):
                    act.wait_ge(nmx_done, h + 1)
                    A.activation(prob[h % 2][:, 0:P], prob[h % 2][:, 0:P], ACT.Exp, bias=nmx[:, h, 0:1],
                                 accum_out=rsum[:, h, 0:1]).then_inc(p_done, 1)
                    A.activation(prob[h % 2][:, P:], prob[h % 2][:, P:], ACT.Exp, bias=nmx[:, h, 1:2],
                                 accum_out=rsum[:, h, 1:2]).then_inc(p_done, 1)

                def attn_turn(h):
                    act.wait_ge(pt_ready, h + 1)
                    if h >= 2:
                        act.wait_ge(pv_done, h - 1)
                    A.activation(probT[h % 2], bank[4][:, 0:384], ACT.Copy).then_inc(pt_evac, 1)

                def attn_out(p):
                    act.wait_ge(pv_done, 2 * p + 2)
                    A.activation(qT[:, p, :], bank[5][:, 0:SEQ], ACT.Copy).then_inc(ob_evac, 1)

                attn_exp(0)
                for h in range(HEADS):
                    if h + 1 < HEADS:
                        attn_exp(h + 1)
                    attn_turn(h)
                    if h % 2:
                        attn_out(h // 2)
                act.wait_ge(ob_evac, 3)
                for p in range(3):
                    out_hi(5 + p, qT[:, p, :], 9 if p == 0 else 10)
                group_std(2, DB)
                layer_norm(1)

                prologue_splits(1)
                ffn(1)
                layer_norm(2)
                act.drain().then_inc(layer_arrived, 1)
                act.wait_ge(layer_open, L + 1)

        @block.vector
        def _(vec):
            V = nc.vector
            vec.wait_ge(const_pool, 11)
            V.tensor_scalar(gbit[:, :], gidx[:, :], 4, 1, ALU.logical_shift_right, ALU.bitwise_and).then_inc(const_vec, 1)
            vec.wait_ge(const_vec, 1)
            V.tensor_scalar(oddg[:, 1:2], gbit[:, :], 1.0, None, ALU.mult).then_inc(const_vec, 1)
            vec.wait_ge(const_vec, 2)
            V.tensor_scalar(oddg[:, 0:1], oddg[:, 1:2], -1.0, 1.0, ALU.mult, ALU.add).then_inc(const_vec, 1)
            vec.sem_inc(lo_done, CREDIT)
            for e in range(4):
                vec.wait_ge(x0_hi, e + 1)
                dst = (slice(None), slice(4 * (e % 2), 4 * (e % 2) + 4), slice((e // 2) * P, (e // 2 + 1) * P))
                V.tensor_tensor(xT_lo[dst], bank[4 + e][:, :].rearrange("p (a n) -> p a n", a=4),
                                xT_hi[dst].bitcast(F32), ALU.subtract).then_inc(x0_lo, 1)

            def split_lo(L, pos0, step, n):
                vec.wait_ge(hi_done, used(L, step + pos0))
                s = pos0 % RING
                V.tensor_tensor(wlo[:, s, 0:n], raw[:, s, 0:n], whi[:, s, 0:n].bitcast(F32), ALU.subtract)\
                    .then_inc(lo_done, 1)

            with vec.Fori(0, DEPTH) as L:
                def prologue_splits(f):
                    for r in range(LEAD):
                        split_lo(L, FFN_BASE[f] + r, 0, 8 * PC)

                def hidden(n_done, up_used, bnk):
                    vec.wait_ge(silu_done, n_done + 1)
                    vec.wait_ge(pieces_used, up_used)
                    V.tensor_tensor(hid, silu, bank[bnk][:, :], ALU.mult).then_inc(hid_done, 1)

                def hidden_lo(n_done, half):
                    vec.wait_ge(hid_hi, n_done + 1)
                    V.tensor_tensor(act_lo[:, half:half + 2, :], hid.rearrange("p (a n) -> p a n", a=2),
                                    act_hi[:, half:half + 2, :].bitcast(F32), ALU.subtract).then_inc(hid_lo, 1)

                def ffn_pair(f, q, i):
                    last = isinstance(i, int)
                    g, u, d = pair_pos(f, q)

                    def ahead(pos):
                        rel = pos + LEAD - FFN_BASE[f] + (6 * i if last else 0)
                        if rel >= FFN_N and f == 1:
                            return
                        split_lo(L, pos + LEAD, i * 6, 8 * PC)
                    ahead(g)
                    ahead(u)
                    vec.wait_ge(hid_lo, i * 2 + (PAIRS * f + q + 1))
                    hidden(i * 2 + (PAIRS * f + q + 1), used(L, i * 6 + u), 6 + (q + 1) % 2)
                    ahead(d)
                    hidden_lo(i * 2 + (PAIRS * f + q + 1), 2 * ((q + 1) % 2))

                def ffn(f):
                    b = FFN_BASE[f]
                    split_lo(L, b + LEAD, 0, 8 * PC)
                    split_lo(L, b + 1 + LEAD, 0, 8 * PC)
                    if f:
                        vec.wait_ge(hid_lo, PAIRS)
                    hidden(PAIRS * f, used(L, b + 1), 6)
                    hidden_lo(PAIRS * f, 0)
                    if f == 0:
                        params()
                    with vec.Fori(0, HALVES - 1) as i:
                        for q in (0, 1):
                            ffn_pair(f, q, i)
                    for q in (0, 1):
                        ffn_pair(f, q, HALVES - 1)
                    if f == 0:
                        split_lo(L, b + FFN_N - 1 + LEAD, 0, 8 * PC)

                ln = [0]
                pv = [0]

                def step(ins):
                    pv[0] += 1
                    ins.then_inc(par_v, 1)
                    vec.wait_ge(par_v, pv[0])

                def log1p(run, e, t, z, z2, acc):
                    run(V.tensor_scalar(t, e, 2.0, None, ALU.add))
                    run(V.reciprocal(t, t))
                    run(V.tensor_tensor(z, e, t, ALU.mult))
                    run(V.tensor_tensor(z2, z, z, ALU.mult))
                    run(V.tensor_scalar(acc, z2, 1.0 / 15.0, None, ALU.mult))
                    for k in (13, 11, 9, 7, 5, 3):
                        run(V.scalar_tensor_tensor(acc, acc, 1.0 / k, z2, ALU.add, ALU.mult))
                    run(V.scalar_tensor_tensor(acc, acc, 1.0, z, ALU.add, ALU.mult))
                    run(V.tensor_scalar(acc, acc, 2.0, None, ALU.mult))

                def params():
                    vec.wait_ge(params_loaded, 16 * N_PARAM_DMAS)
                    V.tensor_copy(parR[96:104, :].rearrange("p (g s) -> p g s", g=2),
                                  dtrow[96:104, :].rearrange("p (g o) -> p g o", o=1).to_broadcast([8, 2, 64]))\
                        .then_inc(dt_spread, 1)
                    vec.wait_ge(par_turned, 1)
                    V.tensor_copy(par[:, 0:NPAR], bank[7][:, 0:NPAR]).then_inc(par_ready, 1)
                    vec.wait_ge(par_ready, 1)
                    re, im = par[:, ROW["a_re"]:ROW["a_re"] + 8], par[:, ROW["a_im"]:ROW["a_im"] + 8]
                    q = lambda n: pq[:, n, :]
                    vec.wait_ge(par_a, 1)
                    step(V.tensor_tensor(q(1), re, q(0), ALU.mult))
                    step(V.tensor_tensor(q(2), im, q(0), ALU.mult))
                    big = 1.5 * 2.0 ** 23
                    step(V.tensor_scalar(q(5), q(2), 1.0 / (2 * math.pi), big, ALU.mult, ALU.add))
                    step(V.tensor_scalar(q(5), q(5), -big, None, ALU.add))
                    c1 = 6.28125
                    c2 = float.fromhex("0x1.fbp-10")
                    c3 = 2 * math.pi - c1 - c2
                    for c in (c1, c2, c3):
                        step(V.scalar_tensor_tensor(q(2), q(5), -c, q(2), ALU.mult, ALU.add))
                    step(V.tensor_scalar(q(6), q(2), 0.5, math.pi / 2, ALU.mult, ALU.min))
                    step(V.tensor_scalar(q(6), q(6), -math.pi / 2, None, ALU.max))
                    step(V.scalar_tensor_tensor(q(7), q(6), -1.0, q(6), ALU.mult, ALU.max))
                    step(V.tensor_scalar(q(7), q(7), -1.0, math.pi / 2, ALU.mult, ALU.add))
                    assert pv[0] == PAR_V_ANGLE, pv
                    r = lambda n: rg[:, n, :]
                    lam = par[:, ROW["lam"]:ROW["lam"] + 3]
                    vec.wait_ge(par_a, 3)
                    step(V.tensor_scalar(r(2), lam, -1.0, 0.0, ALU.mult, ALU.max))
                    log1p(step, r(1), r(3), r(4), r(5), r(6))
                    step(V.tensor_tensor(r(6), r(6), r(2), ALU.add))
                    step(V.tensor_scalar(r(13), r(6), RG_C, None, ALU.mult))
                    step(V.tensor_scalar(r(14), r(6), -RG_C, None, ALU.mult))
                    vec.wait_ge(par_a, 7)
                    step(V.scalar_tensor_tensor(q(12), q(8), -2.0, q(8), ALU.mult, ALU.mult))
                    step(V.tensor_scalar(q(10), q(12), 1.0, None, ALU.add))
                    step(V.scalar_tensor_tensor(q(11), q(8), 2.0, q(9), ALU.mult, ALU.mult))
                    step(V.scalar_tensor_tensor(q(13), q(3), 1.0, q(4), ALU.add, ALU.mult))
                    step(V.tensor_tensor(q(13), q(13), q(10), ALU.mult))
                    step(V.tensor_tensor(q(13), q(13), q(12), ALU.add))
                    step(V.tensor_tensor(q(14), q(3), q(11), ALU.mult))
                    step(V.tensor_tensor(q(15), re, re, ALU.mult))
                    step(V.tensor_tensor(q(16), im, im, ALU.mult))
                    step(V.tensor_tensor(q(15), q(15), q(16), ALU.add))
                    step(V.reciprocal(q(15), q(15)))
                    step(V.tensor_tensor(q(16), q(13), re, ALU.mult))
                    step(V.tensor_tensor(q(17), q(14), im, ALU.mult))
                    step(V.tensor_tensor(q(16), q(16), q(17), ALU.add))
                    step(V.tensor_tensor(q(20), q(16), q(15), ALU.mult))
                    step(V.tensor_tensor(q(18), q(14), re, ALU.mult))
                    step(V.tensor_tensor(q(19), q(13), im, ALU.mult))
                    step(V.tensor_tensor(q(18), q(18), q(19), ALU.subtract))
                    step(V.tensor_tensor(q(21), q(18), q(15), ALU.mult))
                    assert pv[0] == PAR_V_DONE, pv

                def lnstep(ins):
                    ln[0] += 1
                    ins.then_inc(ln_v, 1)

                def settle():
                    vec.wait_ge(ln_v, ln[0])

                def layer_norm(n):
                    if n == 0:
                        vec.wait_ge(tab_step, TAB_DONE)
                    for t in range(TT):
                        if n != 1:
                            f = n // 2
                            vec.wait_ge(xtok_step, XTOK_SCALED[n])
                            if t == 0:
                                vec.wait_ge(y0_ready, f + 1)
                            else:
                                vec.wait_ge(pieces_used, used(L, FFN_BASE[f] + FFN_N - 1))
                            for h in range(2):
                                xs = xtok[:, t, h * 512:(h + 1) * 512]
                                lnstep(V.scalar_tensor_tensor(xs, bank[2 * t + h][:, :], 0.5, xs, ALU.mult, ALU.add))
                            settle()
                        else:
                            vec.wait_ge(proj_evac, 12)
                        for h in range(2):
                            lnstep(V.bn_stats(bn[:, t, h, :], xtok[:, t, h * 512:(h + 1) * 512]))
                        settle()
                        V.bn_aggr(mv[:, t, :], bn[:, t, :, :].rearrange("p a b -> p (a b)")).then_inc(mv_ready, 1)
                    for t in range(TT):
                        vec.wait_ge(std_ready, TT * n + t + 1)
                        lnstep(V.reciprocal(rstd[:, t:t + 1], std[:, t:t + 1]))
                        settle()
                        vec.wait_ge(mv_ready, TT * n + t + 1)
                        V.tensor_scalar(xn[:, t, :], xtok[:, t, :], mv[:, t, 0:1], rstd[:, t:t + 1],
                                        ALU.subtract, ALU.mult).then_inc(xn_ready, 1)
                    for t in range(TT):
                        for b in range(2):
                            e = 4 * n + 2 * t + b
                            vec.wait_ge(xT_affine, e + 1)
                            dst = (slice(None), slice(4 * b, 4 * b + 4), slice(t * P, (t + 1) * P))
                            V.tensor_copy(xT_hi[dst], xT_f[:, b, :, :]).then_inc(xT_hi_done, 1)
                            vec.wait_ge(xT_hi_done, e + 1)
                            V.tensor_tensor(xT_lo[dst], xT_f[:, b, :, :], xT_hi[dst].bitcast(F32), ALU.subtract)\
                                .then_inc(xT_lo_done, 1)

                prologue_splits(0)
                ffn(0)
                layer_norm(0)

                def ahead(m):
                    pos = MIX_BASE + m + LEAD
                    if m + LEAD < MIX_N:
                        split_lo(L, pos, 0, width(pos))

                def conv(f):
                    vec.wait_ge(z_evac, 3 + f)
                    V.tensor_scalar(xa[:, f, :], ax[:, f, 0:SEQ], prow("conv_w", f), prow("conv_b", f),
                                    ALU.mult, ALU.add).then_inc(conv_step, 1)
                    for k in range(1, 4):
                        vec.wait_ge(conv_step, 4 * f + k)
                        V.scalar_tensor_tensor(xa[:, f, :], ax[:, f, k:k + SEQ], prow("conv_w", 3 * k + f),
                                               xa[:, f, :], ALU.mult, ALU.add).then_inc(conv_step, 1)

                def s5_in(i):
                    vec.wait_ge(bu_ready, i + 1)
                    if i == 0:
                        vec.wait_ge(tab_step, TAB_DONE)
                        vec.wait_ge(xtok_step, XTOK_AFFINE[0])
                        vec.wait_ge(xT_turned, 4)
                    else:
                        vec.wait_ge(gin_done, 2 * i)
                    bu = bank[6 + i % 2][:, :].rearrange("p (a n) -> p a n", a=2)
                    cb = ec[:, i:i + 1, :].to_broadcast([P, 2, SEQ])
                    sbr = es[:, i:i + 1, :].to_broadcast([P, 2, SEQ])
                    V.tensor_tensor(s5_t[:, 0:2, :], bu, cb, ALU.mult).then_inc(bu_mul, 1)
                    V.tensor_tensor(s5_t[:, 2:4, :], bu, sbr, ALU.mult).then_inc(bu_mul, 1)

                def s5_out(i):
                    vec.wait_ge(gin_done, 2 * i + 2)
                    if i:
                        vec.wait_ge(s5_rot, 2 * i)
                    for r in range(2):
                        V.tensor_tensor_scan(gs[:, r, :], pq[:, 3, i:i + 1].to_broadcast([P, SEQ]),
                                             gin[:, i % 2, r, :], 0.0, ALU.mult, ALU.add).then_inc(s5_scan, 1)
                    vec.wait_ge(s5_scan, 2 * i + 2)
                    if i:
                        vec.wait_ge(h_done, 2 * i)
                    cb = ec[:, i:i + 1, :].to_broadcast([P, 2, SEQ])
                    sbr = es[:, i:i + 1, :].to_broadcast([P, 2, SEQ])
                    V.tensor_tensor(s5_m[:, 0:2, :], gs[:, :, :], cb, ALU.mult).then_inc(s5_rot, 1)
                    V.tensor_tensor(s5_m[:, 2:4, :], gs[:, :, :], sbr, ALU.mult).then_inc(s5_rot, 1)

                rgn = [0]

                def rgstep(ins, wait=True):
                    rgn[0] += 1
                    ins.then_inc(rg_v, 1)
                    if wait:
                        vec.wait_ge(rg_v, rgn[0])

                def rg_mid():
                    vec.wait_ge(decay_done, 6)
                    rgstep(V.tensor_tensor(osq[:, :, :], av[:, :, :], av[:, :, :], ALU.mult))
                    rgstep(V.scalar_tensor_tensor(th[:, :, :], osq[:, :, :], 1.0, th[:, :, :], ALU.add, ALU.mult),
                           wait=False)
                    assert rgn[0] == RG_V_OM
                    vec.wait_ge(conv_step, 12)
                    rgstep(V.tensor_tensor(ig[:, :, :], ig[:, :, :], xa[:, :, :], ALU.mult))

                def rg_end():
                    vec.wait_ge(sqrt_done, 1)
                    rgstep(V.tensor_tensor(ig[:, :, :], ig[:, :, :], th[:, :, :], ALU.mult))
                    for f in range(3):
                        rgstep(V.tensor_tensor_scan(xa[:, f, :], av[:, f, :], ig[:, f, :], 0.0, ALU.mult, ALU.add),
                               wait=f == 2)
                    vec.wait_ge(z_evac, 8)
                    rgstep(V.tensor_tensor(gg[:, :, :], gg[:, :, :], xa[:, :, :], ALU.mult), wait=False)
                    assert rgn[0] == RG_V_DONE

                fn_ = [0]

                def fstep(ins):
                    fn_[0] += 1
                    ins.then_inc(f_v, 1)
                    vec.wait_ge(f_v, fn_[0])

                def forget():
                    vec.wait_ge(f_evac, 2)
                    fstep(V.tensor_tensor(fx[:, 0], flog[:, :, :],
                                          bf[:, :].rearrange("p (o n) -> p o n", o=1).to_broadcast([P, TT, HEADS]),
                                          ALU.add))
                    fstep(V.tensor_scalar(fx[:, 3], fx[:, 0], -1.0, 0.0, ALU.mult, ALU.max))

                def forget_log():
                    vec.wait_ge(f_a, 2)
                    log1p(fstep, fx[:, 2], fx[:, 4], fx[:, 5], fx[:, 6], fx[:, 7])
                    fstep(V.tensor_tensor(fx[:, 7], fx[:, 7], fx[:, 3], ALU.add))
                    fstep(V.tensor_scalar(logf[:, :, :], fx[:, 7], -1.0, None, ALU.mult))
                    assert fn_[0] == F_V_DONE, fn_

                ahead(0)
                ahead(1)
                conv(0)
                s5_in(0)
                ahead(2)
                conv(1)
                s5_out(0)
                s5_in(1)
                ahead(3)
                conv(2)
                s5_out(1)
                s5_in(2)
                ahead(4)
                s5_out(2)
                s5_in(3)
                forget()
                ahead(5)
                s5_out(3)
                s5_in(4)
                forget_log()
                rg_mid()
                ahead(6)
                s5_out(4)
                s5_in(5)
                rg_end()
                ahead(7)
                s5_out(5)
                s5_in(6)
                ahead(8)
                s5_out(6)
                s5_in(7)
                s5_out(7)
                vec.wait_ge(y_done, S5_TILES)
                vec.wait_ge(s5_rot, 16)
                for m in range(2):
                    V.scalar_tensor_tensor(gs[:, m, :], uT[:, m, :], prow("d", m), bank[5][:, m * SEQ:(m + 1) * SEQ],
                                           ALU.mult, ALU.add).then_inc(ys_step, 1)

                an = [0]

                def attn_logits(h):
                    vec.wait_ge(s_ready, h + 1)
                    if h >= 2:
                        vec.wait_ge(pt_ready, h - 1)
                    else:
                        vec.wait_ge(h_done, 16)
                    S = bank[6 + h % 2]
                    V.tensor_tensor_reduce(prob[h % 2][:, 0:P], S[:, 0:P], mask[:, P:], 1.0, -3e38, ALU.add, ALU.max,
                                           mx[:, h, 0:1]).then_inc(l_done, 1)
                    V.tensor_tensor_reduce(prob[h % 2][:, P:], S[:, P:384], mask[:, :], 1.0, -3e38, ALU.add, ALU.max,
                                           mx[:, h, 1:2]).then_inc(l_done, 1)
                    vec.wait_ge(l_done, 2 * h + 2)
                    V.tensor_scalar(nmx[:, h, :], mx[:, h, :], -1.0, None, ALU.mult).then_inc(nmx_done, 1)

                def attn_norm(h):
                    vec.wait_ge(p_done, 2 * h + 2)
                    V.reciprocal(rrec[:, h, :], rsum[:, h, :]).then_inc(pn_step, 1)
                    vec.wait_ge(pn_step, 3 * h + 1)
                    V.tensor_scalar(prob[h % 2][:, 0:P], prob[h % 2][:, 0:P], rrec[:, h, 0:1], None, ALU.mult)\
                        .then_inc(pn_step, 1)
                    V.tensor_scalar(prob[h % 2][:, P:], prob[h % 2][:, P:], rrec[:, h, 1:2], None, ALU.mult)\
                        .then_inc(pn_step, 1)

                def out_lo(tile, src):
                    vec.wait_ge(o_hi, tile + 1)
                    g = {0: 6, 1: 7}.get(tile, tile - 2)
                    V.scalar_tensor_tensor(act_lo[:, tile % 4, :], src, prow("mix_g", g),
                                           act_hi[:, tile % 4, :].bitcast(F32), ALU.mult, ALU.subtract)\
                        .then_inc(o_lo, 1)

                def group_rstd(g):
                    vec.wait_ge(gstd_done, g + 1)
                    V.reciprocal(grstd[:, g, :], gstd[:, g, :]).then_inc(grstd_done, 1)

                def proj_add(g):
                    vec.wait_ge(grstd_done, g + 1)
                    if g == 0:
                        vec.wait_ge(xtok_step, XTOK_SCALED[1])
                    else:
                        vec.wait_ge(proj_evac, 4 * g)
                    for q in range(4):
                        if q < 3:
                            vec.wait_ge(proj_ready, 3 * g + q + 1)
                        else:
                            vec.wait_ge(pieces_used, used(L, MIX_BASE + (9, 10, 12)[g]))
                        xs = xtok[:, q // 2, (q % 2) * 512:(q % 2 + 1) * 512]
                        V.scalar_tensor_tensor(xs, bank[q][:, :], grstd[:, g, q // 2:q // 2 + 1], xs,
                                               ALU.mult, ALU.add).then_inc(proj_evac, 1)

                vec.wait_ge(glu_sig, 1)
                for m in range(2):
                    V.tensor_tensor(uT[:, m, :], gs[:, m, :], gin[:, 0, m, :], ALU.mult).then_inc(oc_done, 1)
                vec.wait_ge(oc_done, 2)
                out_lo(0, uT[:, 0, :])
                out_lo(1, uT[:, 1, :])
                out_lo(2, gg[:, 0, :])
                out_lo(3, gg[:, 1, :])
                group_rstd(0)
                proj_add(0)
                ahead(9)
                out_lo(4, gg[:, 2, :])
                group_rstd(1)
                attn_logits(0)
                attn_logits(1)
                ahead(10)
                attn_norm(0)
                for h in range(1, HEADS):
                    if h + 1 < HEADS:
                        attn_logits(h + 1)
                    attn_norm(h)
                    if h == 2:
                        proj_add(1)
                for p in range(3):
                    vec.wait_ge(ob_evac, p + 1)
                    out_lo(5 + p, qT[:, p, :])
                group_rstd(2)
                proj_add(2)
                layer_norm(1)

                prologue_splits(1)
                ffn(1)
                layer_norm(2)
                vec.drain().then_inc(layer_arrived, 1)
                vec.wait_ge(layer_open, L + 1)

        @block.tensor
        def _(pe):
            T = nc.tensor
            pe.sem_inc(pieces_used, CREDIT)

            def mm3(out, a_hi, a_lo, b_hi, b_lo, first, last):
                T.matmul(out, a_hi, b_hi, start=first, stop=False)
                T.matmul(out, a_hi, b_lo, start=False, stop=False)
                return T.matmul(out, a_lo, b_hi, start=False, stop=last)

            def turn(dst, src):
                return T.transpose(dst, src, ident[:, :])

            pe.wait_ge(const_pool, 14)
            pe.wait_ge(x_loaded, 16)
            for t in range(TT):
                for b in range(2):
                    for k in range(4):
                        ins = turn(bank[4 + 2 * t + b][:, k * P:(k + 1) * P], xtok[:, t, (4 * b + k) * P:(4 * b + k + 1) * P])
                    ins.then_inc(x0_transposed, 1)
            pe.wait_ge(x0_lo, 4)

            with pe.Fori(0, DEPTH) as L:
                def features(pos0, step, bnk, before=None):
                    pe.wait_ge(lo_done, used(L, step + pos0))
                    hi, lo = piece(whi, pos0, 8, PC), piece(wlo, pos0, 8, PC)
                    for ft in range(2):
                        for k in range(KD):
                            c = slice(ft * P, (ft + 1) * P)
                            ins = mm3(bank[bnk][:, ft * SEQ:(ft + 1) * SEQ], hi[:, k, c], lo[:, k, c],
                                      xT_hi[:, k, :], xT_lo[:, k, :], k == 0, k == KD - 1)
                    ins.then_inc(pieces_used, 1)

                def down(pos0, step, half, n_hid, first, last, f):
                    pe.wait_ge(hid_lo, n_hid)
                    pe.wait_ge(lo_done, used(L, step + pos0))
                    hi, lo = piece(whi, pos0, 2, DM), piece(wlo, pos0, 2, DM)
                    for t in range(TT):
                        for h in range(2):
                            for k in range(2):
                                tok = slice(t * P, (t + 1) * P)
                                col = slice(h * 512, (h + 1) * 512)
                                ins = mm3(bank[2 * t + h][:, :], act_hi[:, half + k, tok], act_lo[:, half + k, tok],
                                          hi[:, k, col], lo[:, k, col], first and k == 0, last and k == 1)
                        if last and t == 0:
                            ins.then_inc(y0_ready, 1)
                    ins.then_inc(pieces_used, 1)

                def ffn_pair(f, q, i):
                    g, u, d = pair_pos(f, q)
                    n = i * 2 + (PAIRS * f + q)
                    par_ = (q + 1) % 2
                    pe.wait_ge(hid_done, n)
                    features(g, i * 6, 4 + par_)
                    features(u, i * 6, 6 + par_)
                    down(d, i * 6, 2 * (q % 2), n + 1, False, False, f)

                def ffn(f):
                    b = FFN_BASE[f]
                    features(b, 0, 4)
                    features(b + 1, 0, 6)
                    if f == 0:
                        pe.wait_ge(dt_spread, 1)
                        turn(bank[7][:, 0:P], parR[:, :]).then_inc(par_turned, 1)
                        pe.wait_ge(par_ready, 1)
                    def first_pair():
                        g, u, d = pair_pos(f, 0)
                        features(g, 0, 5)
                        features(u, 0, 7)
                        down(d, 0, 0, PAIRS * f + 1, True, False, f)
                        g, u, d = pair_pos(f, 1)
                        pe.wait_ge(hid_done, PAIRS * f + 1)
                        features(g, 0, 4)
                        features(u, 0, 6)
                        down(d, 0, 2, PAIRS * f + 2, False, False, f)
                    first_pair()
                    with pe.Fori(1, HALVES) as i:
                        for q in (0, 1):
                            ffn_pair(f, q, i)
                    down(b + FFN_N - 1, 0, 0, PAIRS * (f + 1), False, True, f)

                def turn_rows(n):
                    for t in range(TT):
                        pe.wait_ge(xn_ready, TT * n + t + 1)
                        if n == 0 and t == 1:
                            pe.wait_ge(bc_ready, 2)
                        for b in range(2):
                            for k in range(4):
                                ins = turn(bank[4 + 2 * t + b][:, k * P:(k + 1) * P],
                                           xn[:, t, (4 * b + k) * P:(4 * b + k + 1) * P])
                            ins.then_inc(xT_turned, 1)
                    pe.wait_ge(xT_lo_done, 4 * (n + 1))

                ffn(0)
                pe.wait_ge(hid_done, PAIRS)
                pe.wait_ge(tab_step, TAB_MATS)
                for q in range(2):
                    for r in range(2):
                        ins = turn(bank[7][:, (2 * q + r) * P:(2 * q + r + 1) * P],
                                   bexp[:, r, 4 * q:4 * q + 4, :].rearrange("p a b -> p (a b)"))
                ins.then_inc(bc_turned, 1)
                for q in range(2):
                    for r in range(2):
                        ins = turn(bank[6][:, (2 * q + r) * P:(2 * q + r + 1) * P],
                                   cexp[:, q, r, :, :].rearrange("p a b -> p (a b)"))
                ins.then_inc(bc_turned, 1)
                turn_rows(0)

                def z_free(e):
                    if e >= 4:
                        pe.wait_ge(z_evac, e - 3)

                def z_piece(m):
                    pos = MIX_BASE + m
                    n = width(pos) // 8
                    pe.wait_ge(lo_done, used(L, pos))
                    hi, lo = piece(whi, pos, 8, n), piece(wlo, pos, 8, n)
                    for h in range(2):
                        e = 2 * m + h
                        z_free(e)
                        for k in range(KD):
                            if e in V_EVENTS:
                                c = slice(h * P, (h + 1) * P)
                                ins = mm3(bank[e % 4][:, 0:n], xT_hi[:, k, c], xT_lo[:, k, c], hi[:, k, :], lo[:, k, :],
                                          k == 0, k == KD - 1)
                            else:
                                c = slice(h * P, (h + 1) * P)
                                ins = mm3(bank[e % 4][:, 0:SEQ], hi[:, k, c], lo[:, k, c], xT_hi[:, k, :], xT_lo[:, k, :],
                                          k == 0, k == KD - 1)
                        ins.then_inc(z_half if h == 0 else pieces_used, 1)

                def bu(i):
                    if i == 0:
                        pe.wait_ge(z_evac, 2)
                    if i >= 2:
                        pe.wait_ge(bu_mul, 2 * i - 2)
                    rows = slice(32 * (i % 4), 32 * (i % 4) + 32)
                    for r in range(2):
                        ins = T.matmul(bank[6 + i % 2][:, r * SEQ:(r + 1) * SEQ], bT[rows, 2 * (i // 4) + r, :],
                                       uT[rows, i // 4, :], start=True, stop=True)
                    ins.then_inc(bu_ready, 1)

                def y(i):
                    pe.wait_ge(h_done, 2 * i + 2)
                    rows = slice(32 * (i % 4), 32 * (i % 4) + 32)
                    dst = bank[5][rows, (i // 4) * SEQ:(i // 4 + 1) * SEQ]
                    T.matmul(dst, cT[:, 2 * (i // 4), rows], hh[:, i % 2, 0, :], start=True, stop=False)
                    T.matmul(dst, cT[:, 2 * (i // 4) + 1, rows], hh[:, i % 2, 1, :], start=False, stop=True)\
                        .then_inc(y_done, 1)

                def gates(f):
                    pe.wait_ge(conv_step, 4 * f + 4)
                    if f:
                        pe.wait_ge(gate_sig, 2 * f)
                    for a in range(2):
                        ins = T.matmul(bank[4][:, a * SEQ:(a + 1) * SEQ], wrg[:, a, f, :], xa[:, f, :], start=True, stop=True)
                    ins.then_inc(gates_ready, 1)

                def forget_sums():
                    pe.wait_ge(f_v, F_V_DONE)
                    pe.wait_ge(gate_sig, 6)
                    T.matmul(bank[4][0:HEADS, 0:SEQ], logf[:, 0, :], tri[:, :], start=True, stop=False)
                    T.matmul(bank[4][0:HEADS, P:SEQ], logf[:, 1, :], tri[:, 0:P], start=False, stop=True)\
                        .then_inc(c_ready, 1)

                def scores(h):
                    if h == 0:
                        pe.wait_ge(z_evac, 18)
                        pe.wait_ge(c_loaded, 32)
                        pe.wait_ge(bu_mul, 2 * S5_TILES)
                    if h >= 2:
                        pe.wait_ge(l_done, 2 * h - 2)
                    rows = slice(64 * (h % 2), 64 * (h % 2) + 64)
                    S = bank[6 + h % 2]
                    for t in range(2):
                        q = slice(t * P, (t + 1) * P)
                        n = (t + 1) * P
                        dst = S[:, t * P:t * P + n]
                        T.matmul(dst, qT[rows, h // 2, q], kT[rows, h // 2, 0:n], start=True, stop=False)
                        ins = T.matmul(dst, ec[0:2, h, q], es[0:2, h, 0:n], start=False, stop=True)
                    ins.then_inc(s_ready, 1)

                def turn_probs(h):
                    pe.wait_ge(pn_step, 3 * h + 3)
                    if h == 0:
                        pe.wait_ge(gstd_done, 2)
                    else:
                        pe.wait_ge(pt_evac, h)
                    for b in range(3):
                        ins = turn(bank[4][:, b * P:(b + 1) * P], prob[h % 2][:, b * P:(b + 1) * P])
                    ins.then_inc(pt_ready, 1)

                def values(h):
                    pe.wait_ge(pt_evac, h + 1)
                    if h % 2 == 0 and h:
                        pe.wait_ge(ob_evac, h // 2)
                    if h == 0:
                        pe.wait_ge(ys_step, 2)
                    rows = slice(64 * (h % 2), 64 * (h % 2) + 64)
                    cols = slice(64 * h, 64 * h + 64)
                    pT = probT[h % 2]
                    T.matmul(bank[5][rows, 0:P], vv[:, 0, cols], pT[:, 0:P], start=True, stop=True)
                    T.matmul(bank[5][rows, P:SEQ], vv[:, 0, cols], pT[:, P:2 * P], start=True, stop=False)
                    T.matmul(bank[5][rows, P:SEQ], vv[:, 1, cols], pT[:, 2 * P:], start=False, stop=True)\
                        .then_inc(pv_done, 1)

                def glu():
                    pe.wait_ge(ys_gelu, 1)
                    pe.wait_ge(z_evac, 15)
                    for m in range(2):
                        for k in range(2):
                            ins = T.matmul(bank[2][:, m * SEQ:(m + 1) * SEQ], wglu[:, k, m * P:(m + 1) * P], gs[:, k, :],
                                           start=k == 0, stop=k == 1)
                    ins.then_inc(glu_ready, 1)

                def square_sums(g, n, tiles_before):
                    pe.wait_ge(o_sq, tiles_before + n)
                    if g == 0:
                        pe.wait_ge(c_evac, 2)
                    else:
                        pe.wait_ge(gstd_done, g)
                    if g == 2:
                        pe.wait_ge(pt_evac, HEADS)
                    for t in range(TT):
                        for k in range(n):
                            ins = T.matmul(bank[4][:, 384 + t:385 + t], osq[:, k, t * P:(t + 1) * P], ones[:, 0:1],
                                           start=k == 0, stop=k == n - 1)
                    ins.then_inc(ss_ready, 1)

                def project(g, tiles):
                    pe.wait_ge(o_lo, tiles[-1][0] + 1)
                    pe.wait_ge(lo_done, used(L, MIX_BASE + tiles[-1][1]))
                    for q in range(4):
                        if g:
                            pe.wait_ge(proj_evac, 4 * (g - 1) + q + 1)
                        elif q == 2:
                            pe.wait_ge(glu_sig, 1)
                        tok = slice((q // 2) * P, (q // 2 + 1) * P)
                        col = slice((q % 2) * 512, (q % 2 + 1) * 512)
                        for n, (tile, m, half) in enumerate(tiles):
                            hi, lo = piece(whi, MIX_BASE + m, 2, DM), piece(wlo, MIX_BASE + m, 2, DM)
                            ins = mm3(bank[q][:, :], act_hi[:, tile % 4, tok], act_lo[:, tile % 4, tok],
                                      hi[:, half, col], lo[:, half, col], n == 0, n == len(tiles) - 1)
                            if g == 2 and q == 3 and n == 0:
                                ins.then_inc(pieces_used, 1)
                        ins.then_inc(proj_ready if q < 3 else pieces_used, 1)

                z_piece(0)
                z_piece(1)
                bu(0)
                bu(1)
                z_piece(2)
                gates(0)
                z_piece(3)
                bu(2)
                gates(1)
                z_piece(4)
                y(0)
                bu(3)
                gates(2)
                z_piece(5)
                y(1)
                bu(4)
                z_piece(6)
                forget_sums()
                y(2)
                bu(5)
                z_piece(7)
                y(3)
                bu(6)
                z_piece(8)
                y(4)
                bu(7)
                y(5)
                y(6)
                y(7)
                scores(0)
                scores(1)
                glu()
                square_sums(0, 2, 0)
                project(0, [(0, 9, 0), (1, 9, 1)])
                square_sums(1, 3, 2)
                project(1, [(2, 10, 0), (3, 10, 1), (4, 11, 0)])
                for h in range(HEADS):
                    turn_probs(h)
                    values(h)
                    if h + 2 < HEADS:
                        scores(h + 2)
                square_sums(2, 3, 5)
                project(2, [(5, 11, 1), (6, 12, 0), (7, 12, 1)])
                turn_rows(1)

                ffn(1)
                turn_rows(2)
                pe.drain().then_inc(layer_arrived, 1)
                pe.wait_ge(layer_open, L + 1)


def build(nc, shapes, out_shape):
    w = {}
    for name, shape in shapes.items():
        w[name] = nc.dram_tensor(f"in_{name}", shape, F32, kind="ExternalInput").ap()
    out = nc.dram_tensor("out", out_shape, F32, kind="ExternalOutput").ap()
    trunk(nc, w.pop("x"), w, out)


def kernel(**inputs):
    import numpy as np
    from concourse import bacc
    from concourse.bass_utils import run_bass_kernel_spmd

    nc = bacc.Bacc("TRN2", target_bir_lowering=False, num_devices=1)
    arrays = {name: np.ascontiguousarray(a) for name, a in inputs.items()}
    build(nc, {name: a.shape for name, a in arrays.items()}, arrays["x"].shape)
    result = run_bass_kernel_spmd(nc, [{f"in_{name}": a for name, a in arrays.items()}], core_ids=[0])
    return result.results[0]["out"]
```

```python
from contextlib import ExitStack
import math

import concourse.bass as bass
from concourse import mybir

ALU = mybir.AluOpType
ACT = mybir.ActivationFunctionType
F32 = mybir.dt.float32
F32R = mybir.dt.float32r
I32 = mybir.dt.int32

P = 128
DEPTH, SEQ, DM, DFF = 2, 256, 1024, 2816
KD = DM // P
TT = SEQ // P
DA = DB = 384
DC = 256
HEADS, HD = 6, 64
CGROUP, CSTATE = 16, 64
S5_TILES = (DC // CGROUP) * CSTATE // P
NIN = 2 * DA + 3 * DB + HEADS + DC
ALPHA = (2 * DEPTH) ** 0.25
LN_EPS, RMS_EPS, RG_C = 1e-5, 1e-6, 8.0

PC = 256
PAIRS = DFF // PC
RING = 3
FFN_N = 3 * PAIRS
MIX_N = 13
LAYER_N = 2 * FFN_N + MIX_N
FFN_BASE = (0, FFN_N + MIX_N)
MIX_BASE = FFN_N
LEAD = 2
TURN = MIX_BASE + 10


def slot(pos):
    return (pos if pos < TURN else pos - 1) % RING


def before(pos):
    return next(q for q in range(pos - 1, pos - LAYER_N, -1) if slot(q % LAYER_N) == slot(pos))


SLOT_USES = [sum(slot(q) == s for q in range(LAYER_N)) for s in range(RING)]
CREDIT = 3
HALVES = (PAIRS - 1) // 2

ZPIECES = [4 * DA, 4 * DA + PC, NIN - DC, 3 * PC, 4 * PC, 5 * PC, 0, PC, 2 * PC]
WOUT_ROWS = [3 * PC, 0, PC, 2 * PC]
VT_W = DB - PC + HEADS

ROW = {}
_at = 0
for _name, _n in (("a_re", 8), ("a_im", 8), ("ln1_g", 8), ("ln1_b", 8), ("ln2_g", 8), ("ln2_b", 8),
                  ("ln3_g", 8), ("ln3_b", 8), ("conv_w", 12), ("conv_b", 3), ("b_a", 3), ("b_x", 3),
                  ("lam", 3), ("mix_g", 8), ("log_dt", 8), ("d", 2)):
    ROW[_name] = _at
    _at += _n
NPAR = _at

N_PARAM_DMAS = 26
PAR_V_ANGLE = 11
PAR_V_DONE = 47
LN_BANKS = [[(4, 5), (6, 7)], [(4, 5), (0, 1)], [(4, 5), (0, 1)]]
TAB_MATS = 12
TAB_DONE = TAB_MATS + 2 + 11 * 8
ACT_TILES = 5
RG_V_OM = 1
RG_V_DONE = 7
F_V_DONE = 17
XTOK_SCALED = (2, 8, 14)
XTOK_AFFINE = (6, 12)


def trunk(nc, x, w, out):
    ctx = ExitStack()
    with ctx:
        ctx.enter_context(nc.allow_non_contiguous_dma(reason="small parameters"))

        def sb(name, shape, dt=F32):
            return ctx.enter_context(nc.sbuf_tensor(name, shape, dt))

        def ps(name):
            return ctx.enter_context(nc.psum_tensor(name, [P, 512], F32))

        raw = sb("raw", [P, RING, 8 * PC])
        whi = sb("whi", [P, RING, 8 * PC], F32R)
        wlo = sb("wlo", [P, RING, 8 * PC], F32R)
        xT_hi = sb("xT_hi", [P, KD, SEQ], F32R)
        xT_lo = sb("xT_lo", [P, KD, SEQ], F32R)
        xT_f = sb("xT_f", [P, 2, 4, P])
        xtok = sb("xtok", [P, TT, DM])
        xn = sb("xn", [P, TT, DM])
        lngb = sb("lngb", [P, 2, DM])
        act_hi = sb("act_hi", [P, ACT_TILES, SEQ], F32R)
        act_lo = sb("act_lo", [P, ACT_TILES, SEQ], F32R)
        bn = sb("bn", [P, TT, 2, 6])
        mv = sb("mv", [P, TT, 2])
        std = sb("std", [P, TT])
        rstd = sb("rstd", [P, TT])
        ident = sb("ident", [P, P])
        mask = sb("mask", [P, SEQ])
        tri = sb("tri", [P, SEQ])
        ones = sb("ones", [P, 2])
        eps = sb("eps", [P, 2])
        gidx = sb("gidx", [P, 1], I32)
        gbit = sb("gbit", [P, 1], I32)
        oddg = sb("oddg", [P, 2])
        parR = sb("parR", [P, P])
        par = sb("par", [P, P])
        dtrow = sb("dtrow", [P, 2])
        ec = sb("ec", [P, S5_TILES, SEQ])
        es = sb("es", [P, S5_TILES, SEQ])
        pq = sb("pq", [P, 24, 8])
        rg = sb("rg", [P, 16, 3])
        wp = sb("wp", [P, 5, 8])
        bnat = sb("bnat", [P, 2, 8, CGROUP])
        cnat = sb("cnat", [P, 2, 2, CSTATE])
        bexp = sb("bexp", [P, 2, 8, 2 * CGROUP])
        cexp = sb("cexp", [P, 2, 2, 2, CSTATE])
        bT = sb("bT", [P, 4, P])
        cT = sb("cT", [P, 4, P])
        wrg = sb("wrg", [P, 2, 3, P])
        wglu = sb("wglu", [P, 2, DC])
        bf = sb("bf", [P, HEADS])
        ax = sb("ax", [P, 3, SEQ + 3])
        gg = sb("gg", [P, 3, SEQ])
        qT = sb("qT", [P, 3, SEQ])
        kT = sb("kT", [P, 3, SEQ])
        vv = sb("vv", [P, TT, DB])
        uT = sb("uT", [P, 2, SEQ])
        xa = sb("xa", [P, 3, SEQ])
        ig = sb("ig", [P, 3, SEQ])
        av = sb("av", [P, 3, SEQ])
        th = sb("th", [P, 3, SEQ])
        gin = sb("gin", [P, 2, 2, SEQ])
        gs = sb("gs", [P, 2, SEQ])
        hh = sb("hh", [P, 2, 2, SEQ])
        osq = sb("osq", [P, 3, SEQ])
        flog = sb("flog", [P, TT, HEADS])
        fx = sb("fx", [P, 8, TT, HEADS])
        logf = sb("logf", [P, TT, HEADS])
        crow = sb("crow", [P, 2, SEQ])
        mx = sb("mx", [P, HEADS, 2])
        nmx = sb("nmx", [P, HEADS, 2])
        rsum = sb("rsum", [P, HEADS, 2])
        rrec = sb("rrec", [P, HEADS, 2])
        gstd = sb("gstd", [P, 3, TT])
        grstd = sb("grstd", [P, 3, TT])

        silu = kT[:, 0:2, :].rearrange("p a n -> p (a n)")
        hid = qT[:, 0:2, :].rearrange("p a n -> p (a n)")
        btmp = xa[:, 0:2, :].rearrange("p a (b c) -> p (a b) c", c=CGROUP).rearrange("p (a b) c -> p a b c", a=4)
        s5_t = xn[:, 0, :].rearrange("p (a n) -> p a n", a=4)
        s5_m = xn[:, 1, :].rearrange("p (a n) -> p a n", a=4)
        prob = [lngb[:, 0, i * 384:(i + 1) * 384] for i in range(2)]
        probT = [lngb[:, 1, i * 384:(i + 1) * 384] for i in range(2)]
        cq, ck = (xT_f[:, i, :, :].rearrange("p (a b) n -> p a (b n)", a=2) for i in range(2))
        squared = (gs, osq, ig)

        bank = [ps(f"bank{i}") for i in range(8)]

        def sem(name):
            return ctx.enter_context(nc.semaphore(name))

        x_loaded = [sem(f"x_loaded{t}") for t in range(TT)]
        const_pool = sem("const_pool")
        const_vec = sem("const_vec")
        raw_loaded = [sem(f"raw_loaded{s}") for s in range(RING)]
        hi_done = sem("hi_done")
        lo_done = sem("lo_done")
        pieces_used = sem("pieces_used")
        lngb_loaded = sem("lngb_loaded")
        layer_arrived = sem("layer_arrived")
        loads_begun = sem("loads_begun")
        layer_closed = sem("layer_closed")
        layer_open = sem("layer_open")
        params_loaded = sem("params_loaded")
        x0_transposed = sem("x0_transposed")
        x_in_hi = sem("x_in_hi")
        x_in_lo = sem("x_in_lo")
        rows_final = sem("rows_final")
        stored = sem("stored")
        table_loaded = sem("table_loaded")

        local = []

        def lsem(name):
            s = sem(name)
            local.append(s)
            return s

        dt_spread = lsem("dt_spread")
        par_turned = lsem("par_turned")
        par_ready = lsem("par_ready")
        par_v = lsem("par_v")
        par_a = lsem("par_a")
        tab_step = lsem("tab_step")
        bc_turned = lsem("bc_turned")
        bc_ready = lsem("bc_ready")
        silu_done = lsem("silu_done")
        hid_done = lsem("hid_done")
        hid_hi = lsem("hid_hi")
        hid_lo = lsem("hid_lo")
        y_ready = lsem("y_ready")
        ln_v = lsem("ln_v")
        mv_ready = lsem("mv_ready")
        std_ready = lsem("std_ready")
        xn_ready = lsem("xn_ready")
        xT_turned = lsem("xT_turned")
        xT_affine = lsem("xT_affine")
        xT_hi_done = lsem("xT_hi_done")
        xT_lo_done = lsem("xT_lo_done")
        xT_lo_first = lsem("xT_lo_first")
        xtok_step = lsem("xtok_step")
        z_half = lsem("z_half")
        z_evac = lsem("z_evac")
        gate_gelu = lsem("gate_gelu")
        f_evac = lsem("f_evac")
        conv_first = lsem("conv_first")
        conv_step = lsem("conv_step")
        gates_ready = lsem("gates_ready")
        gate_sig = lsem("gate_sig")
        decay_tanh = lsem("decay_tanh")
        decay_done = lsem("decay_done")
        rg_v = lsem("rg_v")
        sqrt_done = lsem("sqrt_done")
        bu_ready = lsem("bu_ready")
        bu_mul = lsem("bu_mul")
        gin_done = lsem("gin_done")
        s5_scan = lsem("s5_scan")
        s5_rot = lsem("s5_rot")
        h_done = lsem("h_done")
        y_done = lsem("y_done")
        ys_step = lsem("ys_step")
        ys_gelu = lsem("ys_gelu")
        glu_ready = lsem("glu_ready")
        glu_sig = lsem("glu_sig")
        oc_done = lsem("oc_done")
        f_v = lsem("f_v")
        f_a = lsem("f_a")
        c_ready = lsem("c_ready")
        c_evac = lsem("c_evac")
        c_ones = lsem("c_ones")
        c_loaded = lsem("c_loaded")
        s_ready = lsem("s_ready")
        l_done = lsem("l_done")
        nmx_done = lsem("nmx_done")
        p_done = lsem("p_done")
        rrec_done = lsem("rrec_done")
        pn_done = lsem("pn_done")
        pt_ready = lsem("pt_ready")
        pt_evac = lsem("pt_evac")
        pv_done = lsem("pv_done")
        ob_evac = lsem("ob_evac")
        o_hi = lsem("o_hi")
        o_lo = lsem("o_lo")
        o_sq = lsem("o_sq")
        ss_ready = lsem("ss_ready")
        gstd_done = lsem("gstd_done")
        grstd_done = lsem("grstd_done")
        proj_ready = lsem("proj_ready")
        proj_evac = lsem("proj_evac")
        nums = [s.num for s in local]
        assert nums == list(range(nums[0], nums[0] + len(nums))), nums
        local_range = range(nums[0], nums[0] + len(nums))

        def used(L, pos):
            return L * LAYER_N + pos + 1 + CREDIT

        def slot_before(L, pos0, step):
            return used(L, step + before(pos0))

        def loaded(L, pos0, step, turns):
            done = sum(slot(q) == slot(pos0) for q in range(pos0 + 1))
            return (L * SLOT_USES[slot(pos0)] + turns + done) * 16

        gate_w = [w[f"ffn{f}_w_gate"].rearrange("l (k p) (j n) -> l j p k n", p=P, n=PC) for f in (1, 2)]
        up_w = [w[f"ffn{f}_w_up"].rearrange("l (k p) (j n) -> l j p k n", p=P, n=PC) for f in (1, 2)]
        down_w = [w[f"ffn{f}_w_down"].rearrange("l (j k p) n -> l j p k n", p=P, k=2) for f in (1, 2)]
        win = w["w_in"].rearrange("l (k p) n -> l p k n", p=P)
        wout = w["w_out"].rearrange("l (k p) n -> l p k n", p=P)

        def pair_pos(f, q):
            b = FFN_BASE[f] + 2 + 3 * q
            return b, b + 1, b + 2

        def piece(t, pos, k, n):
            return t[:, slot(pos), 0:k * n].rearrange("p (k n) -> p k n", n=n)

        def prow(name, n):
            return par[:, ROW[name] + n:ROW[name] + n + 1]

        def last_rows_read(engine, L, n, t, half):
            if (n, t) == (2, 1):
                engine.wait_ge(x_in_lo, L * 4 + 4 + 2)
            elif half == 0 and n and (n, t) > (1, 0):
                engine.wait_ge(xT_lo_first, 2 * n + t - 2)
            elif n or t:
                engine.wait_ge(xT_lo_done, 2 * t if n == 0 else 2 + 2 * n + t)

        LN_NAMES = ("ln1", "ln2", "ln3")
        V_EVENTS = (0, 1, 2, 3)

        def z_bank(e):
            return e if e < 4 else e % 2

        def proj_bank(g, q):
            return 4 + q if g == 2 and q >= 2 else (0, 1, 3)[(4 * g + q) % 3]

        block = ctx.enter_context(nc.Block())

        @block.sync
        def _(sp):
            rows_in = x[0].rearrange("(t p) n -> p t n", p=P)
            for t in range(TT):
                sp.dma_start(xtok[:, t, :], rows_in[:, t, :]).then_inc(x_loaded[t], 16)

            def load(L, pos0, step, turns, src, k, n):
                sp.wait_ge(lo_done, slot_before(L, pos0, step))
                sp.sem_inc(loads_begun, 1)
                sp.dma_start(piece(raw, pos0, k, n), src).then_inc(raw_loaded[slot(pos0)], 16)

            def small(L):
                rows = {"a_re": "s5_a_re", "a_im": "s5_a_im", "lam": "rg_lambda", "ln1_g": "ln1_g", "ln1_b": "ln1_b",
                        "ln2_g": "ln2_g", "ln2_b": "ln2_b", "ln3_g": "ln3_g", "ln3_b": "ln3_b", "conv_w": "conv_w",
                        "conv_b": "conv_b", "b_a": "rg_b_a", "b_x": "rg_b_x", "mix_g": "mix_norm_g", "d": "s5_d"}
                todo = [(dtrow[96:104, :], w["s5_log_dt"].rearrange("l (t g) -> l t g", g=2)[L])]
                for name, key in rows.items():
                    src = w[key]
                    if name == "conv_w":
                        src = src.rearrange("l k (t n) -> l (k t) n", n=P)
                    elif key in ("s5_a_re", "s5_a_im"):
                        src = src.rearrange("l (r g) s -> l r (g s)", g=2)
                    else:
                        src = src.rearrange("l (r n) -> l r n", n=P)
                    todo.append((parR[ROW[name]:ROW[name] + src.shape[1], :], src[L]))
                for r, c in enumerate(("re", "im")):
                    todo.append((bnat[:, r, :, :], w[f"s5_b_{c}"].rearrange("l (t g) s c -> l (g s) t c", g=2)[L]))
                    todo.append((cnat[:, r, :, :], w[f"s5_c_{c}"].rearrange("l (q g) c s -> l (g c) q s", q=2)[L]))
                for a, key in enumerate(("rg_w_a", "rg_w_x")):
                    for h in range(2):
                        todo.append((wrg[64 * h:64 * h + 64, a, :, 64 * h:64 * h + 64],
                                     w[key].rearrange("l (t h) i o -> l h i t o", h=2)[L, h]))
                todo.append((wglu[:, :, :], w["s5_w_glu"].rearrange("l (k p) n -> l p k n", p=P)[L]))
                todo.append((bf[:, :], w["fox_b_f"][L].rearrange("(o n) -> o n", o=1).to_broadcast([P, HEADS])))
                assert len(todo) == N_PARAM_DMAS
                return todo

            def ffn(L, f):
                b = FFN_BASE[f]
                todo = small(L) if f == 0 else []

                def some_params(n):
                    for dst, src in todo[:n]:
                        sp.dma_start(dst, src).then_inc(params_loaded, 16)
                    del todo[:n]

                def turn_loads(i):
                    for q in (0, 1):
                        g, u, d = pair_pos(f, q)
                        load(L, g, i * 6, i * 2, gate_w[f][L, i * 2 + (q + 1)], 8, PC)
                        some_params(7)
                        load(L, u, i * 6, i * 2, up_w[f][L, i * 2 + (q + 1)], 8, PC)
                        some_params(7)
                        load(L, d, i * 6, i * 2, down_w[f][L, i * 2 + q], 2, DM)
                        some_params(7)

                load(L, b, 0, 0, gate_w[f][L, 0], 8, PC)
                load(L, b + 1, 0, 0, up_w[f][L, 0], 8, PC)
                if f == 0:
                    turn_loads(0)
                with sp.Fori(1 - f, HALVES) as i:
                    turn_loads(i)
                load(L, b + FFN_N - 1, 0, 0, down_w[f][L, PAIRS - 1], 2, DM)

            with sp.Fori(0, DEPTH) as L:
                ffn(L, 0)
                for m, col in enumerate(ZPIECES):
                    load(L, MIX_BASE + m, 0, 0, win[L, :, :, col:col + PC], 8, PC)
                for m, row in enumerate(WOUT_ROWS):
                    load(L, MIX_BASE + len(ZPIECES) + m, 0, 0, wout[L, :, row // P:row // P + 2, :], 2, DM)
                ffn(L, 1)
            rows_out = out[0].rearrange("(t p) n -> p t n", p=P)
            for t in range(TT):
                sp.wait_ge(rows_final, TT * (DEPTH - 1) + t + 1)
                sp.dma_start(rows_out[:, t, :], xtok[:, t, :]).then_inc(stored, 16)
            sp.wait_ge(stored, 16 * TT)

        @block.gpsimd
        def _(pool):
            pool.memset(ident[:, :], 0.0).then_inc(const_pool, 1)
            pool.memset(mask[:, :], 0.0).then_inc(const_pool, 1)
            pool.memset(tri[:, :], 1.0).then_inc(const_pool, 1)
            pool.memset(ones[:, :], 1.0).then_inc(const_pool, 1)
            pool.memset(eps[:, 0:1], LN_EPS).then_inc(const_pool, 1)
            pool.memset(eps[:, 1:2], RMS_EPS).then_inc(const_pool, 1)
            pool.memset(ax[:, :, 0:3], 0.0).then_inc(const_pool, 1)
            pool.memset(parR[:, :], 0.0).then_inc(const_pool, 1)
            pool.memset(wrg[:, :, :, :], 0.0).then_inc(const_pool, 1)
            pool.memset(bexp[:, :, :, :], 0.0).then_inc(const_pool, 1)
            pool.iota(gidx[:, :], [[0, 1]], base=0, channel_multiplier=1).then_inc(const_pool, 1)
            pool.wait_ge(const_pool, 11)
            pool.affine_select(out=ident[:, :], in_=ident[:, :], compare_op=ALU.not_equal, fill=1.0, base=0,
                               pattern=[[-1, P]], channel_multiplier=1).then_inc(const_pool, 1)
            pool.affine_select(out=mask[:, P:], in_=mask[:, P:], compare_op=ALU.is_ge, fill=-1e30, base=0,
                               pattern=[[-1, P]], channel_multiplier=1).then_inc(const_pool, 1)
            pool.affine_select(out=tri[:, :], in_=tri[:, :], compare_op=ALU.is_ge, fill=0.0, base=0,
                               pattern=[[1, SEQ]], channel_multiplier=-1).then_inc(const_pool, 1)

            pool.sem_inc(layer_open, 1)
            with pool.Fori(0, DEPTH) as L:
                steps = [0]

                def mark_x(ins):
                    steps[0] += 1
                    ins.then_inc(xtok_step, 1)

                def load_gb(n):
                    for h, k in enumerate("gb"):
                        src = w[f"{LN_NAMES[n]}_{k}"][L]
                        src = src.rearrange("(o n) -> o n", o=1).to_broadcast([P, DM])
                        pool.dma_start(lngb[:, h, :], src).then_inc(lngb_loaded, 16)

                def scale_residual():
                    if steps[0]:
                        pool.wait_ge(xtok_step, steps[0])
                    for t in range(TT):
                        mark_x(pool.tensor_scalar(xtok[:, t, :], xtok[:, t, :], ALPHA, 1.0, ALU.mult, ALU.mult))

                def affine(n):
                    pool.wait_ge(lngb_loaded, L * 96 + 32 * (n + 1))
                    for t in range(TT):
                        pool.wait_ge(xn_ready, TT * n + t + 1)
                        mark_x(pool.tensor_tensor(xtok[:, t, :], xn[:, t, :], lngb[:, 0, :], ALU.mult))
                        pool.wait_ge(xtok_step, steps[0])
                        ins = pool.tensor_tensor(xtok[:, t, :], xtok[:, t, :], lngb[:, 1, :], ALU.add)
                        if n < 2:
                            mark_x(ins)
                        else:
                            ins.then_inc(rows_final, 1)
                    if n < 2:
                        pool.wait_ge(xtok_step, steps[0])

                for t in range(TT):
                    pool.wait_ge(x_loaded[t], 16)
                pool.wait_ge(x0_transposed, 4)
                scale_residual()
                load_gb(0)

                tabs = [0]

                def tab(ins, settle=True):
                    tabs[0] += 1
                    ins.then_inc(tab_step, 1)
                    if settle:
                        pool.wait_ge(tab_step, tabs[0])

                pool.wait_ge(const_vec, 3)
                pool.wait_ge(dt_spread, 1)
                for r in range(2):
                    for half in range(2):
                        tab(pool.tensor_scalar(cexp[:, :, r, half, :], cnat[:, r, :, :], oddg[:, half:half + 1],
                                               1.0 if r == 0 else -1.0, ALU.mult, ALU.mult), settle=False)
                pool.wait_ge(par_v, PAR_V_DONE)
                cr = pq[:, 20, :].rearrange("p (a o) -> p a o", o=1).to_broadcast([P, 8, CGROUP])
                ci = pq[:, 21, :].rearrange("p (a o) -> p a o", o=1).to_broadcast([P, 8, CGROUP])
                tab(pool.tensor_tensor(btmp[:, 0], bnat[:, 0], cr, ALU.mult), settle=False)
                tab(pool.tensor_tensor(btmp[:, 1], bnat[:, 1], ci, ALU.mult), settle=False)
                tab(pool.tensor_tensor(btmp[:, 2], bnat[:, 1], cr, ALU.mult), settle=False)
                tab(pool.tensor_tensor(btmp[:, 3], bnat[:, 0], ci, ALU.mult))
                for half in range(2):
                    rows = slice(64 * half, 64 * half + 64)
                    cols = slice(CGROUP * half, CGROUP * half + CGROUP)
                    tab(pool.tensor_tensor(bexp[rows, 0, :, cols], btmp[rows, 0], btmp[rows, 1], ALU.subtract))
                    tab(pool.tensor_tensor(bexp[rows, 1, :, cols], btmp[rows, 2], btmp[rows, 3], ALU.add))
                tab(pool.memset(ec[:, :, 0:1], 1.0), settle=False)
                tab(pool.memset(es[:, :, 0:1], 0.0))
                cw, sw = pq[:, 10, :], pq[:, 11, :]
                n = 1
                while n < SEQ:
                    cb = cw.rearrange("p (a o) -> p a o", o=1).to_broadcast([P, 8, n])
                    sbr = sw.rearrange("p (a o) -> p a o", o=1).to_broadcast([P, 8, n])
                    tab(pool.tensor_tensor(ec[:, :, n:2 * n], ec[:, :, 0:n], cb, ALU.mult), settle=False)
                    tab(pool.tensor_tensor(es[:, :, n:2 * n], es[:, :, 0:n], cb, ALU.mult), settle=False)
                    t0 = xn[:, 0, :].rearrange("p (a n) -> p a n", a=S5_TILES)[:, :, 0:n]
                    t1 = xn[:, 1, :].rearrange("p (a n) -> p a n", a=S5_TILES)[:, :, 0:n]
                    tab(pool.tensor_tensor(t0, es[:, :, 0:n], sbr, ALU.mult), settle=False)
                    tab(pool.tensor_tensor(t1, ec[:, :, 0:n], sbr, ALU.mult))
                    tab(pool.tensor_tensor(ec[:, :, n:2 * n], ec[:, :, n:2 * n], t0, ALU.subtract), settle=False)
                    tab(pool.tensor_tensor(es[:, :, n:2 * n], es[:, :, n:2 * n], t1, ALU.add), settle=False)
                    tab(pool.tensor_tensor(wp[:, 2, :], cw, cw, ALU.mult), settle=False)
                    tab(pool.tensor_tensor(wp[:, 3, :], sw, sw, ALU.mult), settle=False)
                    tab(pool.tensor_tensor(wp[:, 4, :], cw, sw, ALU.mult))
                    tab(pool.tensor_tensor(wp[:, 0, :], wp[:, 2, :], wp[:, 3, :], ALU.subtract), settle=False)
                    tab(pool.tensor_tensor(wp[:, 1, :], wp[:, 4, :], wp[:, 4, :], ALU.add))
                    cw, sw = wp[:, 0, :], wp[:, 1, :]
                    n *= 2
                assert tabs[0] == TAB_DONE, tabs

                affine(0)
                scale_residual()
                pool.wait_ge(xT_lo_done, 4)
                pool.memset(cq[:, :, :], 1.0).then_inc(c_ones, 1)
                pool.memset(ck[:, :, :], 1.0).then_inc(c_ones, 1)

                def attn_scale(h):
                    pool.wait_ge(rrec_done, h + 1)
                    pool.tensor_scalar(prob[h % 2][:, 0:P], prob[h % 2][:, 0:P], rrec[:, h, 0:1], 1.0, ALU.mult,
                                       ALU.mult).then_inc(pn_done, 1)
                    pool.tensor_scalar(prob[h % 2][:, P:], prob[h % 2][:, P:], rrec[:, h, 1:2], 1.0, ALU.mult,
                                       ALU.mult).then_inc(pn_done, 1)

                for i in range(S5_TILES):
                    pool.wait_ge(bu_mul, 2 * i + 2)
                    if i >= 2:
                        pool.wait_ge(s5_scan, 2 * i - 2)
                    pool.tensor_tensor(gin[:, i % 2, 0, :], s5_t[:, 0, :], s5_t[:, 3, :], ALU.add).then_inc(gin_done, 1)
                    pool.tensor_tensor(gin[:, i % 2, 1, :], s5_t[:, 1, :], s5_t[:, 2, :], ALU.subtract)\
                        .then_inc(gin_done, 1)
                    pool.wait_ge(s5_rot, 2 * i + 2)
                    if i >= 2:
                        pool.wait_ge(y_done, i - 1)
                    pool.tensor_tensor(hh[:, i % 2, 0, :], s5_m[:, 0, :], s5_m[:, 3, :], ALU.subtract)\
                        .then_inc(h_done, 1)
                    pool.tensor_tensor(hh[:, i % 2, 1, :], s5_m[:, 1, :], s5_m[:, 2, :], ALU.add).then_inc(h_done, 1)
                    if i in (5, 6):
                        attn_scale(i - 5)
                attn_scale(2)
                attn_scale(3)

                def squares(g, src, n):
                    for t in range(n):
                        if g == 2:
                            pool.wait_ge(ob_evac, t + 1)
                        pool.tensor_tensor(squared[g][:, t, :], src[:, t, :], src[:, t, :], ALU.mult)\
                            .then_inc(o_sq, 1)

                pool.wait_ge(oc_done, 2)
                squares(0, uT, 2)
                attn_scale(4)
                attn_scale(5)
                pool.wait_ge(rg_v, RG_V_DONE)
                squares(1, gg, 3)
                squares(2, qT, 3)
                pool.wait_ge(pv_done, HEADS)
                load_gb(1)

                for t in range(TT):
                    tok = slice(t * P, (t + 1) * P)
                    pool.wait_ge(xT_hi_done, TT + t + 1)
                    pool.tensor_tensor(xT_lo[:, 0:4, tok], xT_f[:, 0, :, :], xT_hi[:, 0:4, tok].bitcast(F32),
                                       ALU.subtract).then_inc(xT_lo_first, 1)
                affine(1)
                scale_residual()
                load_gb(2)
                affine(2)
                pool.drain().then_inc(layer_arrived, 1)
                pool.wait_ge(layer_arrived, L * 4 + 4)
                pool.sem_inc(layer_closed, 1)
                pool.sem_clear(local_range)
                pool.sem_inc(layer_open, 1)

        @block.scalar
        def _(act):
            A = nc.scalar

            def split_hi(L, pos0, step, turns, n):
                s = slot(pos0)
                act.wait_ge(raw_loaded[s], loaded(L, pos0, step, turns))
                act.wait_ge(pieces_used, slot_before(L, pos0, step))
                A.activation(whi[:, s, 0:n], raw[:, s, 0:n], ACT.Copy).then_inc(hi_done, 1)

            act.sem_inc(hi_done, CREDIT)
            act.wait_ge(const_pool, 11)
            A.activation(std[:, 0:1], eps[:, 0:1], ACT.Sqrt).then_inc(table_loaded, 1)
            for e in range(4):
                act.wait_ge(x0_transposed, e + 1)
                A.activation(xT_hi[:, 4 * (e % 2):4 * (e % 2) + 4, (e // 2) * P:(e // 2 + 1) * P],
                             bank[4 + e][:, :].rearrange("p (a n) -> p a n", a=4), ACT.Copy).then_inc(x_in_hi, 1)

            with act.Fori(0, DEPTH) as L:
                def ffn_pair(L, f, q, i, params=False):
                    last = isinstance(i, int) and i > 0
                    g, u, d = pair_pos(f, q)
                    i6, i2 = i * 6, i * 2

                    def ahead(pos):
                        rel = pos + LEAD - FFN_BASE[f] + (6 * i if last else 0)
                        if rel >= FFN_N and f == 1:
                            return
                        split_hi(L, pos + LEAD, i6, i2, 8 * PC)
                    ahead(g)
                    if params:
                        exponentials()
                    act.wait_ge(pieces_used, used(L, i6 + g))
                    act.wait_ge(hid_done, i2 + (PAIRS * f + q + 1))
                    A.activation(silu, bank[4 + (q + 1) % 2][:, :], ACT.Silu).then_inc(silu_done, 1)
                    if params:
                        sines()
                    ahead(u)
                    act.wait_ge(hid_done, i2 + (PAIRS * f + q + 2))
                    act.wait_ge(pieces_used, used(L, i6 + (d - 3)))
                    o = 2 * ((q + 1) % 2)
                    A.activation(act_hi[:, o:o + 2, :], hid.rearrange("p (a n) -> p a n", a=2), ACT.Copy)\
                        .then_inc(hid_hi, 1)
                    ahead(d)

                def ffn(f):
                    b = FFN_BASE[f]
                    split_hi(L, b + LEAD, 0, 0, 8 * PC)
                    if f == 0:
                        act.wait_ge(layer_open, L + 1)
                    else:
                        act.wait_ge(hid_done, PAIRS)
                    act.wait_ge(pieces_used, used(L, b))
                    A.activation(silu, bank[4][:, :], ACT.Silu).then_inc(silu_done, 1)
                    split_hi(L, b + 1 + LEAD, 0, 0, 8 * PC)
                    act.wait_ge(hid_done, PAIRS * f + 1)
                    A.activation(act_hi[:, 0:2, :], hid.rearrange("p (a n) -> p a n", a=2), ACT.Copy)\
                        .then_inc(hid_hi, 1)
                    if f == 0:
                        ffn_pair(L, f, 0, 0)
                        ffn_pair(L, f, 1, 0, params=True)
                    with act.Fori(1 - f, HALVES - 1) as i:
                        for q in (0, 1):
                            ffn_pair(L, f, q, i)
                    for q in (0, 1):
                        ffn_pair(L, f, q, HALVES - 1)

                def par_fn(need, out, in_, fn, **kw):
                    act.wait_ge(par_v, need)
                    A.activation(out, in_, fn, **kw).then_inc(par_a, 1)

                def exponentials():
                    act.wait_ge(par_ready, 1)
                    A.activation(pq[:, 0, :], par[:, ROW["log_dt"]:ROW["log_dt"] + 8], ACT.Exp).then_inc(par_a, 1)
                    A.activation(rg[:, 0, :], par[:, ROW["lam"]:ROW["lam"] + 3], ACT.Abs).then_inc(par_a, 1)
                    act.wait_ge(par_a, 2)
                    A.activation(rg[:, 1, :], rg[:, 0, :], ACT.Exp, scale=-1.0).then_inc(par_a, 1)
                    par_fn(1, pq[:, 3, :], pq[:, 1, :], ACT.Exp)
                    par_fn(1, pq[:, 4, :], pq[:, 1, :], ACT.Tanh, scale=0.5)

                def sines():
                    par_fn(PAR_V_ANGLE, pq[:, 8, :], pq[:, 6, :], ACT.Sin)
                    par_fn(PAR_V_ANGLE, pq[:, 9, :], pq[:, 7, :], ACT.Sin)

                def layer_norm(n):
                    g0, b0 = LN_NAMES[n] + "_g", LN_NAMES[n] + "_b"
                    def deviation(t):
                        act.wait_ge(mv_ready, TT * n + t + 1)
                        A.activation(std[:, t:t + 1], mv[:, t, 1:2], ACT.Sqrt, bias=eps[:, 0:1]).then_inc(std_ready, 1)

                    deviation(0)
                    for t in range(TT):
                        if t == 1 and n == 0:
                            split_hi(L, MIX_BASE + 1, 0, 0, 8 * PC)
                        if n != 1 and t == 1:
                            deviation(1)
                        act.wait_ge(xT_turned, 4 * n + 2 * t + 1)
                        last_rows_read(act, L, n, t, 0)
                        for k in range(4):
                            ins = A.activation(xT_f[:, 0, k, :], bank[LN_BANKS[n][t][0]][:, k * P:(k + 1) * P],
                                               ACT.Identity, bias=prow(b0, k), scale=prow(g0, k))
                        ins.then_inc(xT_affine, 1)
                        if (n, t) == (1, 0):
                            deviation(1)
                        act.wait_ge(xT_affine, TT * n + t + 1)
                        A.activation(xT_hi[:, 0:4, t * P:(t + 1) * P], xT_f[:, 0, :, :], ACT.Copy)\
                            .then_inc(xT_hi_done, 1)
                    if n == 1:
                        split_hi(L, FFN_BASE[1] + 1, 0, 0, 8 * PC)

                for r in range(LEAD):
                    split_hi(L, r, 0, 0, 8 * PC)
                ffn(0)
                layer_norm(0)

                def ahead(m):
                    pos = MIX_BASE + m + LEAD
                    split_hi(L, pos, 0, 0, 8 * PC)

                def z_wait(e):
                    if e % 2 == 0:
                        act.wait_ge(z_half, e // 2 + 1)
                    else:
                        act.wait_ge(pieces_used, used(L, MIX_BASE + e // 2))

                def evac(e, dst, fn=ACT.Copy, **kw):
                    z_wait(e)
                    A.activation(dst, bank[z_bank(e)][:, 0:SEQ], fn, **kw).then_inc(z_evac, 1)

                def values_out(t):
                    z_wait(t)
                    A.activation(vv[:, t, 0:PC], bank[t][:, 0:PC], ACT.Copy).then_inc(z_evac, 1)
                    z_wait(2 + t)
                    A.activation(flog[:, t, :], bank[2 + t][:, DB - PC:VT_W], ACT.Copy).then_inc(f_evac, 1)
                    A.activation(vv[:, t, PC:], bank[2 + t][:, 0:DB - PC], ACT.Copy).then_inc(z_evac, 1)

                def conv_tap(f):
                    act.wait_ge(z_evac, 12 + f + 1)
                    A.activation(xa[:, f, :], ax[:, f, 0:SEQ], ACT.Identity, bias=prow("conv_b", f),
                                 scale=prow("conv_w", f)).then_inc(conv_first, 1)

                def gate_sigmoids(f):
                    act.wait_ge(gates_ready, f + 1)
                    A.activation(av[:, f, :], bank[3][:, 0:SEQ], ACT.Sigmoid, bias=prow("b_a", f)).then_inc(gate_sig, 1)
                    A.activation(ig[:, f, :], bank[3][:, SEQ:], ACT.Sigmoid, bias=prow("b_x", f)).then_inc(gate_sig, 1)

                    act.wait_ge(gate_sig, 2 * f + 1)
                    A.activation(th[:, f, :], av[:, f, :], ACT.Tanh, scale=rg[:, 13, f:f + 1]).then_inc(decay_tanh, 1)

                def decays():
                    act.wait_ge(decay_tanh, 3)
                    for f in range(3):
                        A.activation(av[:, f, :], av[:, f, :], ACT.Exp, scale=rg[:, 14, f:f + 1]).then_inc(decay_done, 1)

                def out_hi(tile, src, last_used):
                    if tile >= ACT_TILES:
                        act.wait_ge(ob_evac, tile - ACT_TILES + 1)
                        act.wait_ge(pieces_used, used(L, MIX_BASE + last_used))
                    g = {0: 6, 1: 7}.get(tile, tile - 2)
                    A.activation(act_hi[:, tile % ACT_TILES, :], src, ACT.Copy, scale=prow("mix_g", g)).then_inc(o_hi, 1)

                def group_std(g, n):
                    act.wait_ge(ss_ready, g + 1)
                    A.activation(gstd[:, g, :], bank[2][:, 0:TT], ACT.Sqrt, bias=eps[:, 1:2], scale=1.0 / n)\
                        .then_inc(gstd_done, 1)

                def attn_exp(h):
                    act.wait_ge(nmx_done, h + 1)
                    A.activation(prob[h % 2][:, 0:P], prob[h % 2][:, 0:P], ACT.Exp, bias=nmx[:, h, 0:1],
                                 accum_out=rsum[:, h, 0:1]).then_inc(p_done, 1)
                    A.activation(prob[h % 2][:, P:], prob[h % 2][:, P:], ACT.Exp, bias=nmx[:, h, 1:2],
                                 accum_out=rsum[:, h, 1:2]).then_inc(p_done, 1)

                def attn_turn(h):
                    act.wait_ge(pt_ready, h + 1)
                    if h >= 2:
                        act.wait_ge(pv_done, h - 1)
                    A.activation(probT[h % 2], bank[4][:, 0:384], ACT.Copy).then_inc(pt_evac, 1)

                def attn_out(p):
                    act.wait_ge(pv_done, 2 * p + 2)
                    A.activation(qT[:, p, :], bank[5][:, 0:SEQ], ACT.Copy).then_inc(ob_evac, 1)

                ahead(0)
                values_out(0)
                values_out(1)
                ahead(1)
                for n, (r, dst) in enumerate(((7, bT), (6, cT))):
                    act.wait_ge(bc_turned, n + 1)
                    A.activation(dst[:, :, :].rearrange("p a n -> p (a n)"), bank[r][:, :], ACT.Copy)\
                        .then_inc(bc_ready, 1)
                ahead(2)
                evac(4, uT[:, 0, :])
                evac(5, uT[:, 1, :])
                act.wait_ge(f_v, 1)
                A.activation(fx[:, 1], fx[:, 0], ACT.Abs).then_inc(f_a, 1)
                act.wait_ge(f_a, 1)
                A.activation(fx[:, 2], fx[:, 1], ACT.Exp, scale=-1.0).then_inc(f_a, 1)
                ahead(3)
                evac(6, qT[:, 0, :], scale=HD ** -0.5)
                evac(7, qT[:, 1, :], scale=HD ** -0.5)
                ahead(4)
                evac(8, qT[:, 2, :], scale=HD ** -0.5)
                act.wait_ge(c_ready, 1)
                A.activation(crow[0:HEADS, 0, :], bank[4][0:HEADS, 0:SEQ], ACT.Copy).then_inc(c_evac, 1)
                A.activation(crow[0:HEADS, 1, :], bank[4][0:HEADS, 0:SEQ], ACT.Copy, scale=-1.0).then_inc(c_evac, 1)
                act.wait_ge(c_evac, 2)
                act.wait_ge(c_ones, 2)
                for b in range(2):
                    act.dma_start(cq[0:65:32, b, :], crow[3 * b:3 * b + 3, 0, :]).then_inc(c_loaded, 16)
                    act.dma_start(ck[1:66:32, b, :], crow[3 * b:3 * b + 3, 1, :]).then_inc(c_loaded, 16)
                evac(9, kT[:, 0, :])
                ahead(5)
                evac(10, kT[:, 1, :])
                attn_exp(0)
                evac(11, kT[:, 2, :])
                ahead(6)
                attn_exp(1)
                evac(12, ax[:, 0, 3:])
                attn_turn(0)
                conv_tap(0)
                evac(13, ax[:, 1, 3:])
                conv_tap(1)
                attn_turn(1)
                gate_sigmoids(0)
                ahead(7)
                evac(14, ax[:, 2, 3:])
                conv_tap(2)
                attn_exp(2)
                attn_out(0)
                attn_exp(3)
                gate_sigmoids(1)
                act.wait_ge(ys_step, 2)
                A.activation(gs[:, :, :], gs[:, :, :], ACT.Gelu_apprx_tanh).then_inc(ys_gelu, 1)
                evac(15, gg[:, 0, :])
                attn_turn(2)
                gate_sigmoids(2)
                evac(16, gg[:, 1, :])
                attn_turn(3)
                act.wait_ge(glu_ready, 1)
                A.activation(gin[:, 0, :, :], bank[2][:, :].rearrange("p (a n) -> p a n", a=2), ACT.Sigmoid)\
                    .then_inc(glu_sig, 1)
                decays()
                act.wait_ge(oc_done, 2)
                out_hi(0, uT[:, 0, :], 0)
                out_hi(1, uT[:, 1, :], 0)
                evac(17, gg[:, 2, :])
                act.wait_ge(decay_done, 3)
                A.activation(osq[:, :, :], av[:, :, :], ACT.Square).then_inc(decay_done, 1)
                attn_exp(4)
                attn_exp(5)
                act.wait_ge(rg_v, RG_V_OM)
                A.activation(th[:, :, :], th[:, :, :], ACT.Sqrt).then_inc(sqrt_done, 1)
                group_std(0, DC)
                act.wait_ge(z_evac, 18)
                A.activation(gg[:, :, :], gg[:, :, :], ACT.Gelu_apprx_tanh).then_inc(gate_gelu, 1)
                attn_turn(4)
                attn_out(1)
                ahead(8)
                attn_turn(5)
                act.wait_ge(rg_v, RG_V_DONE)
                for t in range(3):
                    out_hi(2 + t, gg[:, t, :], 0)
                ahead(9)
                group_std(1, DA)
                attn_out(2)
                out_hi(5, qT[:, 0, :], 9)
                out_hi(6, qT[:, 1, :], 9)
                ahead(10)
                out_hi(7, qT[:, 2, :], 10)
                ahead(11)
                group_std(2, DB)
                layer_norm(1)

                ffn(1)
                layer_norm(2)
                act.drain().then_inc(layer_arrived, 1)

        @block.vector
        def _(vec):
            V = nc.vector
            vec.wait_ge(const_pool, 11)
            V.tensor_scalar(gbit[:, :], gidx[:, :], 4, 1, ALU.logical_shift_right, ALU.bitwise_and).then_inc(const_vec, 1)
            vec.wait_ge(const_vec, 1)
            V.tensor_scalar(oddg[:, 1:2], gbit[:, :], 1.0, None, ALU.mult).then_inc(const_vec, 1)
            vec.wait_ge(const_vec, 2)
            V.tensor_scalar(oddg[:, 0:1], oddg[:, 1:2], -1.0, 1.0, ALU.mult, ALU.add).then_inc(const_vec, 1)
            vec.sem_inc(lo_done, CREDIT)
            for e in range(4):
                vec.wait_ge(x_in_hi, e + 1)
                dst = (slice(None), slice(4 * (e % 2), 4 * (e % 2) + 4), slice((e // 2) * P, (e // 2 + 1) * P))
                V.tensor_tensor(xT_lo[dst], bank[4 + e][:, :].rearrange("p (a n) -> p a n", a=4),
                                xT_hi[dst].bitcast(F32), ALU.subtract).then_inc(x_in_lo, 1)

            def split_lo(L, pos0, step, n):
                vec.wait_ge(hi_done, used(L, step + pos0))
                s = slot(pos0)
                V.tensor_tensor(wlo[:, s, 0:n], raw[:, s, 0:n], whi[:, s, 0:n].bitcast(F32), ALU.subtract)\
                    .then_inc(lo_done, 1)

            with vec.Fori(0, DEPTH) as L:
                def hidden(n_done, up_used, bnk):
                    vec.wait_ge(silu_done, n_done + 1)
                    vec.wait_ge(pieces_used, up_used)
                    V.tensor_tensor(hid, silu, bank[bnk][:, :], ALU.mult).then_inc(hid_done, 1)

                def hidden_lo(n_done, half):
                    vec.wait_ge(hid_hi, n_done + 1)
                    V.tensor_tensor(act_lo[:, half:half + 2, :], hid.rearrange("p (a n) -> p a n", a=2),
                                    act_hi[:, half:half + 2, :].bitcast(F32), ALU.subtract).then_inc(hid_lo, 1)

                def ffn_pair(f, q, i, params=False):
                    last = isinstance(i, int) and i > 0
                    g, u, d = pair_pos(f, q)

                    def ahead(pos):
                        rel = pos + LEAD - FFN_BASE[f] + (6 * i if last else 0)
                        if rel >= FFN_N and f == 1:
                            return
                        split_lo(L, pos + LEAD, i * 6, 8 * PC)
                    ahead(g)
                    if params:
                        angles()
                    ahead(u)
                    vec.wait_ge(hid_lo, i * 2 + (PAIRS * f + q + 1))
                    hidden(i * 2 + (PAIRS * f + q + 1), used(L, i * 6 + u), 6 + (q + 1) % 2)
                    if params:
                        softplus()
                    if last and q == 1:
                        hidden_lo(i * 2 + (PAIRS * f + q + 1), 2 * ((q + 1) % 2))
                        ahead(d)
                    else:
                        ahead(d)
                        hidden_lo(i * 2 + (PAIRS * f + q + 1), 2 * ((q + 1) % 2))
                    if params:
                        input_scales()

                def ffn(f):
                    b = FFN_BASE[f]
                    split_lo(L, b + LEAD, 0, 8 * PC)
                    split_lo(L, b + 1 + LEAD, 0, 8 * PC)
                    if f == 0:
                        vec.wait_ge(layer_open, L + 1)
                    else:
                        vec.wait_ge(hid_lo, PAIRS)
                    hidden(PAIRS * f, used(L, b + 1), 6)
                    hidden_lo(PAIRS * f, 0)
                    if f == 0:
                        ffn_pair(f, 0, 0)
                        spread_steps()
                        ffn_pair(f, 1, 0, params=True)
                    with vec.Fori(1 - f, HALVES - 1) as i:
                        for q in (0, 1):
                            ffn_pair(f, q, i)
                    for q in (0, 1):
                        ffn_pair(f, q, HALVES - 1)

                ln = [0]
                pv = [0]

                def step(ins):
                    pv[0] += 1
                    ins.then_inc(par_v, 1)
                    vec.wait_ge(par_v, pv[0])

                def log1p(run, e, t, z, z2, acc):
                    log1p_argument(run, e, t, z, z2, acc)
                    log1p_series(run, z, z2, acc)

                def log1p_argument(run, e, t, z, z2, acc):
                    run(V.tensor_scalar(t, e, 2.0, None, ALU.add))
                    run(V.reciprocal(t, t))
                    run(V.tensor_tensor(z, e, t, ALU.mult))
                    run(V.tensor_tensor(z2, z, z, ALU.mult))
                    run(V.tensor_scalar(acc, z2, 1.0 / 15.0, None, ALU.mult))

                def log1p_series(run, z, z2, acc):
                    for k in (13, 11, 9, 7, 5, 3):
                        run(V.scalar_tensor_tensor(acc, acc, 1.0 / k, z2, ALU.add, ALU.mult))
                    run(V.scalar_tensor_tensor(acc, acc, 1.0, z, ALU.add, ALU.mult))
                    run(V.tensor_scalar(acc, acc, 2.0, None, ALU.mult))

                q = lambda n: pq[:, n, :]
                r = lambda n: rg[:, n, :]
                re, im = par[:, ROW["a_re"]:ROW["a_re"] + 8], par[:, ROW["a_im"]:ROW["a_im"] + 8]

                def spread_steps():
                    vec.wait_ge(params_loaded, L * (16 * N_PARAM_DMAS) + 16 * N_PARAM_DMAS)
                    V.tensor_copy(parR[96:104, :].rearrange("p (g s) -> p g s", g=2),
                                  dtrow[96:104, :].rearrange("p (g o) -> p g o", o=1).to_broadcast([8, 2, 64]))\
                        .then_inc(dt_spread, 1)

                def angles():
                    vec.wait_ge(par_turned, 1)
                    V.tensor_copy(par[:, 0:NPAR], bank[6][:, 0:NPAR]).then_inc(par_ready, 1)
                    vec.wait_ge(par_ready, 1)
                    vec.wait_ge(par_a, 1)
                    step(V.tensor_tensor(q(1), re, q(0), ALU.mult))
                    step(V.tensor_tensor(q(2), im, q(0), ALU.mult))
                    big = 1.5 * 2.0 ** 23
                    step(V.tensor_scalar(q(5), q(2), 1.0 / (2 * math.pi), big, ALU.mult, ALU.add))
                    step(V.tensor_scalar(q(5), q(5), -big, None, ALU.add))
                    c1 = 6.28125
                    c2 = float.fromhex("0x1.fbp-10")
                    c3 = 2 * math.pi - c1 - c2
                    for c in (c1, c2, c3):
                        step(V.scalar_tensor_tensor(q(2), q(5), -c, q(2), ALU.mult, ALU.add))
                    step(V.tensor_scalar(q(6), q(2), 0.5, math.pi / 2, ALU.mult, ALU.min))
                    step(V.tensor_scalar(q(6), q(6), -math.pi / 2, None, ALU.max))
                    step(V.scalar_tensor_tensor(q(7), q(6), -1.0, q(6), ALU.mult, ALU.max))
                    step(V.tensor_scalar(q(7), q(7), -1.0, math.pi / 2, ALU.mult, ALU.add))
                    assert pv[0] == PAR_V_ANGLE, pv

                def softplus():
                    lam = par[:, ROW["lam"]:ROW["lam"] + 3]
                    vec.wait_ge(par_a, 3)
                    step(V.tensor_scalar(r(2), lam, -1.0, 0.0, ALU.mult, ALU.max))
                    log1p(step, r(1), r(3), r(4), r(5), r(6))
                    step(V.tensor_tensor(r(6), r(6), r(2), ALU.add))
                    step(V.tensor_scalar(r(13), r(6), RG_C, None, ALU.mult))
                    step(V.tensor_scalar(r(14), r(6), -RG_C, None, ALU.mult))

                def input_scales():
                    vec.wait_ge(par_a, 7)
                    step(V.scalar_tensor_tensor(q(12), q(8), -2.0, q(8), ALU.mult, ALU.mult))
                    step(V.tensor_scalar(q(10), q(12), 1.0, None, ALU.add))
                    step(V.scalar_tensor_tensor(q(11), q(8), 2.0, q(9), ALU.mult, ALU.mult))
                    step(V.scalar_tensor_tensor(q(13), q(3), 1.0, q(4), ALU.add, ALU.mult))
                    step(V.tensor_tensor(q(13), q(13), q(10), ALU.mult))
                    step(V.tensor_tensor(q(13), q(13), q(12), ALU.add))
                    step(V.tensor_tensor(q(14), q(3), q(11), ALU.mult))
                    step(V.tensor_tensor(q(15), re, re, ALU.mult))
                    step(V.tensor_tensor(q(16), im, im, ALU.mult))
                    step(V.tensor_tensor(q(15), q(15), q(16), ALU.add))
                    step(V.reciprocal(q(15), q(15)))
                    step(V.tensor_tensor(q(16), q(13), re, ALU.mult))
                    step(V.tensor_tensor(q(17), q(14), im, ALU.mult))
                    step(V.tensor_tensor(q(16), q(16), q(17), ALU.add))
                    step(V.tensor_tensor(q(20), q(16), q(15), ALU.mult))
                    step(V.tensor_tensor(q(18), q(14), re, ALU.mult))
                    step(V.tensor_tensor(q(19), q(13), im, ALU.mult))
                    step(V.tensor_tensor(q(18), q(18), q(19), ALU.subtract))
                    step(V.tensor_tensor(q(21), q(18), q(15), ALU.mult))
                    assert pv[0] == PAR_V_DONE, pv

                def lnstep(ins):
                    ln[0] += 1
                    ins.then_inc(ln_v, 1)

                def settle():
                    vec.wait_ge(ln_v, ln[0])

                def proj_add(g, qs):
                    if qs[0] == 0:
                        vec.wait_ge(grstd_done, g + 1)
                        if g == 0:
                            vec.wait_ge(xtok_step, XTOK_SCALED[1])
                        else:
                            vec.wait_ge(proj_evac, 4 * g)
                    for q in qs:
                        if q < 3:
                            vec.wait_ge(proj_ready, 3 * g + q + 1)
                        else:
                            vec.wait_ge(pieces_used, used(L, MIX_BASE + (9, 10, 12)[g]))
                        xs = xtok[:, q // 2, (q % 2) * 512:(q % 2 + 1) * 512]
                        V.scalar_tensor_tensor(xs, bank[proj_bank(g, q)][:, :], grstd[:, g, q // 2:q // 2 + 1], xs,
                                               ALU.mult, ALU.add).then_inc(proj_evac, 1)

                def layer_norm(n):
                    g0, b0 = LN_NAMES[n] + "_g", LN_NAMES[n] + "_b"
                    f = n // 2

                    def residual(t, h):
                        xs = xtok[:, t, h * 512:(h + 1) * 512]
                        if n == 1:
                            proj_add(2, (2 * t + h,))
                            vec.wait_ge(proj_evac, 8 + 2 * t + h + 1)
                        else:
                            if (t, h) < (1, 1):
                                vec.wait_ge(y_ready, 3 * f + 2 * t + h + 1)
                            else:
                                vec.wait_ge(pieces_used, used(L, FFN_BASE[f] + FFN_N - 1))
                            lnstep(V.scalar_tensor_tensor(xs, bank[2 * t + h][:, :], 0.5, xs, ALU.mult, ALU.add))
                            settle()
                        lnstep(V.bn_stats(bn[:, t, h, :], xs))

                    def normalise(t):
                        settle()
                        V.bn_aggr(mv[:, t, :], bn[:, t, :, :].rearrange("p a b -> p (a b)")).then_inc(mv_ready, 1)
                        vec.wait_ge(std_ready, TT * n + t + 1)
                        lnstep(V.reciprocal(rstd[:, t:t + 1], std[:, t:t + 1]))
                        settle()
                        vec.wait_ge(mv_ready, TT * n + t + 1)
                        V.tensor_scalar(xn[:, t, :], xtok[:, t, :], mv[:, t, 0:1], rstd[:, t:t + 1],
                                        ALU.subtract, ALU.mult).then_inc(xn_ready, 1)

                    def feature_rows(t):
                        tok = slice(t * P, (t + 1) * P)
                        vec.wait_ge(xT_turned, 4 * n + 2 * t + 2)
                        last_rows_read(vec, L, n, t, 1)
                        for k in range(4):
                            lnstep(V.tensor_scalar(xT_f[:, 1, k, :], bank[LN_BANKS[n][t][1]][:, k * P:(k + 1) * P],
                                                   prow(g0, 4 + k), prow(b0, 4 + k), ALU.mult, ALU.add))
                        settle()
                        lnstep(V.tensor_copy(xT_hi[:, 4:, tok], xT_f[:, 1, :, :]))
                        settle()

                    def lower_rows(t):
                        tok = slice(t * P, (t + 1) * P)
                        for b in (1, 0) if n != 1 else (1,):
                            if b == 0:
                                vec.wait_ge(xT_hi_done, TT * n + t + 1)
                            rows = slice(4 * b, 4 * b + 4)
                            V.tensor_tensor(xT_lo[:, rows, tok], xT_f[:, b, :, :], xT_hi[:, rows, tok].bitcast(F32),
                                            ALU.subtract).then_inc(xT_lo_done if n < 2 else x_in_lo, 1)

                    if n == 0:
                        vec.wait_ge(tab_step, TAB_DONE)
                    if n != 1:
                        vec.wait_ge(xtok_step, XTOK_SCALED[n])
                    residual(0, 0)
                    residual(0, 1)
                    normalise(0)
                    residual(1, 0)
                    if n == 1:
                        residual(1, 1)
                        normalise(1)
                        feature_rows(0)
                        lower_rows(0)
                    elif n == 0:
                        feature_rows(0)
                        lower_rows(0)
                        residual(1, 1)
                        normalise(1)
                        split_lo(L, MIX_BASE + 1, 0, 8 * PC)
                    else:
                        feature_rows(0)
                        residual(1, 1)
                        normalise(1)
                        lower_rows(0)
                    feature_rows(1)
                    lower_rows(1)
                    if n == 1:
                        split_lo(L, FFN_BASE[1] + 1, 0, 8 * PC)

                for rel in range(LEAD):
                    split_lo(L, rel, 0, 8 * PC)
                ffn(0)
                layer_norm(0)

                def ahead(m):
                    pos = MIX_BASE + m + LEAD
                    split_lo(L, pos, 0, 8 * PC)

                def conv(f):
                    for k in range(1, 4):
                        if k == 1:
                            vec.wait_ge(conv_first, f + 1)
                        else:
                            vec.wait_ge(conv_step, 3 * f + k - 1)
                        V.scalar_tensor_tensor(xa[:, f, :], ax[:, f, k:k + SEQ], prow("conv_w", 3 * k + f),
                                               xa[:, f, :], ALU.mult, ALU.add).then_inc(conv_step, 1)

                def s5_in(i):
                    vec.wait_ge(bu_ready, i + 1)
                    if i == 0:
                        vec.wait_ge(tab_step, TAB_DONE)
                        vec.wait_ge(xtok_step, XTOK_AFFINE[0])
                        vec.wait_ge(xT_turned, 4)
                    else:
                        vec.wait_ge(gin_done, 2 * i)
                    bu = bank[3][:, :].rearrange("p (a n) -> p a n", a=2)
                    cb = ec[:, i:i + 1, :].to_broadcast([P, 2, SEQ])
                    sbr = es[:, i:i + 1, :].to_broadcast([P, 2, SEQ])
                    V.tensor_tensor(s5_t[:, 0:2, :], bu, cb, ALU.mult).then_inc(bu_mul, 1)
                    V.tensor_tensor(s5_t[:, 2:4, :], bu, sbr, ALU.mult).then_inc(bu_mul, 1)

                def s5_out(i):
                    vec.wait_ge(gin_done, 2 * i + 2)
                    if i:
                        vec.wait_ge(s5_rot, 2 * i)
                    for r in range(2):
                        V.tensor_tensor_scan(gs[:, r, :], pq[:, 3, i:i + 1].to_broadcast([P, SEQ]),
                                             gin[:, i % 2, r, :], 0.0, ALU.mult, ALU.add).then_inc(s5_scan, 1)
                    vec.wait_ge(s5_scan, 2 * i + 2)
                    if i:
                        vec.wait_ge(h_done, 2 * i)
                    cb = ec[:, i:i + 1, :].to_broadcast([P, 2, SEQ])
                    sbr = es[:, i:i + 1, :].to_broadcast([P, 2, SEQ])
                    V.tensor_tensor(s5_m[:, 0:2, :], gs[:, :, :], cb, ALU.mult).then_inc(s5_rot, 1)
                    V.tensor_tensor(s5_m[:, 2:4, :], gs[:, :, :], sbr, ALU.mult).then_inc(s5_rot, 1)

                rgn = [0]

                def rgstep(ins, wait=True):
                    rgn[0] += 1
                    ins.then_inc(rg_v, 1)
                    if wait:
                        vec.wait_ge(rg_v, rgn[0])

                def rg_mid():
                    vec.wait_ge(decay_done, 4)
                    rgstep(V.scalar_tensor_tensor(th[:, :, :], osq[:, :, :], 1.0, th[:, :, :], ALU.add, ALU.mult),
                           wait=False)
                    assert rgn[0] == RG_V_OM
                    vec.wait_ge(conv_step, 9)
                    rgstep(V.tensor_tensor(ig[:, :, :], ig[:, :, :], xa[:, :, :], ALU.mult))

                def rg_end():
                    vec.wait_ge(sqrt_done, 1)
                    rgstep(V.tensor_tensor(ig[:, :, :], ig[:, :, :], th[:, :, :], ALU.mult))
                    for f in range(3):
                        rgstep(V.tensor_tensor_scan(xa[:, f, :], av[:, f, :], ig[:, f, :], 0.0, ALU.mult, ALU.add),
                               wait=f == 2)
                    vec.wait_ge(gate_gelu, 1)
                    rgstep(V.tensor_tensor(gg[:, :, :], gg[:, :, :], xa[:, :, :], ALU.mult), wait=False)
                    assert rgn[0] == RG_V_DONE

                fn_ = [0]

                def fstep(ins):
                    fn_[0] += 1
                    ins.then_inc(f_v, 1)
                    vec.wait_ge(f_v, fn_[0])

                def forget():
                    vec.wait_ge(f_evac, 2)
                    fstep(V.tensor_tensor(fx[:, 0], flog[:, :, :],
                                          bf[:, :].rearrange("p (o n) -> p o n", o=1).to_broadcast([P, TT, HEADS]),
                                          ALU.add))
                    fstep(V.tensor_scalar(fx[:, 3], fx[:, 0], -1.0, 0.0, ALU.mult, ALU.max))

                def forget_log():
                    vec.wait_ge(f_a, 2)
                    log1p_argument(fstep, fx[:, 2], fx[:, 4], fx[:, 5], fx[:, 6], fx[:, 7])

                def forget_series():
                    log1p_series(fstep, fx[:, 5], fx[:, 6], fx[:, 7])
                    fstep(V.tensor_tensor(fx[:, 7], fx[:, 7], fx[:, 3], ALU.add))
                    fstep(V.tensor_scalar(logf[:, :, :], fx[:, 7], -1.0, None, ALU.mult))
                    assert fn_[0] == F_V_DONE, fn_

                def s5_sum():
                    vec.wait_ge(y_done, S5_TILES)
                    vec.wait_ge(s5_rot, 16)
                    for m in range(2):
                        V.scalar_tensor_tensor(gs[:, m, :], uT[:, m, :], prow("d", m), bank[2][:, m * SEQ:(m + 1) * SEQ],
                                               ALU.mult, ALU.add).then_inc(ys_step, 1)

                def attn_logits(h):
                    vec.wait_ge(s_ready, h + 1)
                    if h >= 2:
                        vec.wait_ge(pt_ready, h - 1)
                    S = bank[6 + h % 2]
                    V.tensor_tensor_reduce(prob[h % 2][:, 0:P], S[:, 0:P], mask[:, P:], 1.0, -3e38, ALU.add, ALU.max,
                                           mx[:, h, 0:1]).then_inc(l_done, 1)
                    V.tensor_tensor_reduce(prob[h % 2][:, P:], S[:, P:384], mask[:, :], 1.0, -3e38, ALU.add, ALU.max,
                                           mx[:, h, 1:2]).then_inc(l_done, 1)
                    vec.wait_ge(l_done, 2 * h + 2)
                    V.tensor_scalar(nmx[:, h, :], mx[:, h, :], -1.0, None, ALU.mult).then_inc(nmx_done, 1)

                def attn_recip(h):
                    vec.wait_ge(p_done, 2 * h + 2)
                    V.reciprocal(rrec[:, h, :], rsum[:, h, :]).then_inc(rrec_done, 1)

                def out_lo(tile, src):
                    vec.wait_ge(o_hi, tile + 1)
                    g = {0: 6, 1: 7}.get(tile, tile - 2)
                    V.scalar_tensor_tensor(act_lo[:, tile % ACT_TILES, :], src, prow("mix_g", g),
                                           act_hi[:, tile % ACT_TILES, :].bitcast(F32), ALU.mult, ALU.subtract)\
                        .then_inc(o_lo, 1)

                def group_rstd(g):
                    vec.wait_ge(gstd_done, g + 1)
                    V.reciprocal(grstd[:, g, :], gstd[:, g, :]).then_inc(grstd_done, 1)

                ahead(0)
                ahead(1)
                forget()
                ahead(2)
                s5_in(0)
                forget_log()
                s5_out(0)
                s5_in(1)
                ahead(3)
                s5_out(1)
                s5_in(2)
                forget_series()
                s5_out(2)
                s5_in(3)
                ahead(4)
                s5_out(3)
                s5_in(4)
                s5_out(4)
                ahead(5)
                s5_in(5)
                attn_logits(0)
                s5_out(5)
                attn_recip(0)
                s5_in(6)
                attn_logits(1)
                s5_out(6)
                ahead(6)
                attn_recip(1)
                s5_in(7)
                conv(0)
                attn_logits(2)
                s5_out(7)
                conv(1)
                ahead(7)
                attn_recip(2)
                s5_sum()
                attn_logits(3)
                conv(2)
                attn_recip(3)
                attn_logits(4)
                vec.wait_ge(glu_sig, 1)
                for m in range(2):
                    V.tensor_tensor(uT[:, m, :], gs[:, m, :], gin[:, 0, m, :], ALU.mult).then_inc(oc_done, 1)
                vec.wait_ge(oc_done, 2)
                out_lo(0, uT[:, 0, :])
                out_lo(1, uT[:, 1, :])
                attn_recip(4)
                attn_logits(5)
                rg_mid()
                attn_recip(5)
                group_rstd(0)
                proj_add(0, (0, 1))
                rg_end()
                proj_add(0, (2,))
                ahead(8)
                proj_add(0, (3,))
                for t in range(3):
                    out_lo(2 + t, gg[:, t, :])
                ahead(9)
                out_lo(5, qT[:, 0, :])
                out_lo(6, qT[:, 1, :])
                group_rstd(1)
                proj_add(1, (0, 1))
                ahead(10)
                proj_add(1, (2, 3))
                out_lo(7, qT[:, 2, :])
                ahead(11)
                group_rstd(2)
                layer_norm(1)

                ffn(1)
                layer_norm(2)
                vec.drain().then_inc(layer_arrived, 1)

        @block.tensor
        def _(pe):
            T = nc.tensor
            pe.sem_inc(pieces_used, CREDIT)

            def mm3(out, a_hi, a_lo, b_hi, b_lo, first, last):
                T.matmul(out, a_hi, b_hi, start=first, stop=False)
                T.matmul(out, a_hi, b_lo, start=False, stop=False)
                return T.matmul(out, a_lo, b_hi, start=False, stop=last)

            def turn(dst, src):
                return T.transpose(dst, src, ident[:, :])

            pe.wait_ge(const_pool, 14)
            for t in range(TT):
                pe.wait_ge(x_loaded[t], 16)
                for b in range(2):
                    for k in range(4):
                        ins = turn(bank[4 + 2 * t + b][:, k * P:(k + 1) * P], xtok[:, t, (4 * b + k) * P:(4 * b + k + 1) * P])
                    ins.then_inc(x0_transposed, 1)

            with pe.Fori(0, DEPTH) as L:
                def features(pos0, step, bnk, before=None):
                    pe.wait_ge(lo_done, used(L, step + pos0))
                    hi, lo = piece(whi, pos0, 8, PC), piece(wlo, pos0, 8, PC)
                    for ft in range(2):
                        for k in range(KD):
                            c = slice(ft * P, (ft + 1) * P)
                            ins = mm3(bank[bnk][:, ft * SEQ:(ft + 1) * SEQ], hi[:, k, c], lo[:, k, c],
                                      xT_hi[:, k, :], xT_lo[:, k, :], k == 0, k == KD - 1)
                    ins.then_inc(pieces_used, 1)

                def down(pos0, step, half, n_hid, first):
                    pe.wait_ge(hid_lo, n_hid)
                    pe.wait_ge(lo_done, used(L, step + pos0))
                    for t in range(TT):
                        for h in range(2):
                            ins = down_rows(pos0, half, t, h, first, False)
                    ins.then_inc(pieces_used, 1)

                def down_rows(pos0, half, t, h, first, last):
                    hi, lo = piece(whi, pos0, 2, DM), piece(wlo, pos0, 2, DM)
                    tok, col = slice(t * P, (t + 1) * P), slice(h * 512, (h + 1) * 512)
                    for k in range(2):
                        ins = mm3(bank[2 * t + h][:, :], act_hi[:, half + k, tok], act_lo[:, half + k, tok],
                                  hi[:, k, col], lo[:, k, col], first and k == 0, last and k == 1)
                    return ins

                def ffn_pair(f, q, i, with_down=True):
                    g, u, d = pair_pos(f, q)
                    n = i * 2 + (PAIRS * f + q)
                    par_ = (q + 1) % 2
                    pe.wait_ge(hid_done, n)
                    features(g, i * 6, 4 + par_)
                    features(u, i * 6, 6 + par_)
                    if with_down:
                        down(d, i * 6, 2 * (q % 2), n + 1, False)

                def ffn(f):
                    b = FFN_BASE[f]
                    if f == 0:
                        pe.wait_ge(x_in_lo, L * 4 + 4)
                    else:
                        pe.wait_ge(xT_lo_done, 6)
                        pe.wait_ge(xT_lo_first, 2)
                    features(b, 0, 4)
                    features(b + 1, 0, 6)
                    g, u, d = pair_pos(f, 0)
                    features(g, 0, 5)
                    features(u, 0, 7)
                    if f == 0:
                        pe.wait_ge(layer_open, L + 1)
                    down(d, 0, 0, PAIRS * f + 1, True)
                    g, u, d = pair_pos(f, 1)
                    pe.wait_ge(hid_done, PAIRS * f + 1)
                    if f == 0:
                        pe.wait_ge(dt_spread, 1)
                        turn(bank[6][:, 0:P], parR[:, :]).then_inc(par_turned, 1)
                    features(g, 0, 4)
                    if f == 0:
                        pe.wait_ge(par_ready, 1)
                    features(u, 0, 6)
                    down(d, 0, 2, PAIRS * f + 2, False)
                    with pe.Fori(1, HALVES - 1) as i:
                        for q in (0, 1):
                            ffn_pair(f, q, i)
                    ffn_pair(f, 0, HALVES - 1)
                    ffn_pair(f, 1, HALVES - 1, with_down=False)
                    d9, d10 = b + FFN_N - 2, b + FFN_N - 1
                    pe.wait_ge(hid_lo, PAIRS * f + PAIRS - 1)
                    pe.wait_ge(lo_done, used(L, d9))
                    for h in range(2):
                        down_rows(d9, 2, 0, h, False, False)
                    pe.wait_ge(hid_lo, PAIRS * f + PAIRS)
                    pe.wait_ge(lo_done, used(L, d10))
                    for h in range(2):
                        down_rows(d10, 0, 0, h, False, True).then_inc(y_ready, 1)
                    down_rows(d9, 2, 1, 0, False, False)
                    down_rows(d10, 0, 1, 0, False, True).then_inc(y_ready, 1)
                    down_rows(d9, 2, 1, 1, False, False).then_inc(pieces_used, 1)
                    turn_rows(2 * f, 0)
                    down_rows(d10, 0, 1, 1, False, True).then_inc(pieces_used, 1)

                def turn_rows(n, t):
                    pe.wait_ge(xn_ready, TT * n + t + 1)
                    if t == 0 and n != 1:
                        pe.wait_ge(hid_done, PAIRS * (n // 2 + 1))
                    for b in range(2):
                        for k in range(4):
                            ins = turn(bank[LN_BANKS[n][t][b]][:, k * P:(k + 1) * P],
                                       xn[:, t, (4 * b + k) * P:(4 * b + k + 1) * P])
                        ins.then_inc(xT_turned, 1)

                ffn(0)

                def z_free(e):
                    if e >= 4:
                        pe.wait_ge(z_evac, e - 1 if e >= 6 else 3 if e == 5 else 1)

                def z_event(e):
                    pos, h = MIX_BASE + e // 2, e % 2
                    pe.wait_ge(lo_done, used(L, pos))
                    z_free(e)
                    hi, lo = piece(whi, pos, 8, PC), piece(wlo, pos, 8, PC)
                    c = slice(h * P, (h + 1) * P)
                    for k in range(KD):
                        if e in V_EVENTS:
                            ins = mm3(bank[z_bank(e)][:, 0:PC], xT_hi[:, k, c], xT_lo[:, k, c], hi[:, k, :], lo[:, k, :],
                                      k == 0, k == KD - 1)
                        else:
                            ins = mm3(bank[z_bank(e)][:, 0:SEQ], hi[:, k, c], lo[:, k, c], xT_hi[:, k, :], xT_lo[:, k, :],
                                      k == 0, k == KD - 1)
                    ins.then_inc(z_half if h == 0 else pieces_used, 1)

                def bu(i):
                    if i == 0:
                        pe.wait_ge(bc_ready, 2)
                    if i % 4 == 0:
                        pe.wait_ge(z_evac, 5 + i // 4)
                    if i:
                        pe.wait_ge(bu_mul, 2 * i)
                    rows = slice(32 * (i % 4), 32 * (i % 4) + 32)
                    for r in range(2):
                        ins = T.matmul(bank[3][:, r * SEQ:(r + 1) * SEQ], bT[rows, 2 * (i // 4) + r, :],
                                       uT[rows, i // 4, :], start=True, stop=True)
                    ins.then_inc(bu_ready, 1)

                def y(i):
                    pe.wait_ge(h_done, 2 * i + 2)
                    rows = slice(32 * (i % 4), 32 * (i % 4) + 32)
                    dst = bank[2][rows, (i // 4) * SEQ:(i // 4 + 1) * SEQ]
                    T.matmul(dst, cT[:, 2 * (i // 4), rows], hh[:, i % 2, 0, :], start=True, stop=False)
                    T.matmul(dst, cT[:, 2 * (i // 4) + 1, rows], hh[:, i % 2, 1, :], start=False, stop=True)\
                        .then_inc(y_done, 1)

                def gates(f):
                    pe.wait_ge(conv_step, 3 * f + 3)
                    if f:
                        pe.wait_ge(gate_sig, 2 * f)
                    else:
                        pe.wait_ge(bu_mul, 2 * S5_TILES)
                    for a in range(2):
                        ins = T.matmul(bank[3][:, a * SEQ:(a + 1) * SEQ], wrg[:, a, f, :], xa[:, f, :], start=True, stop=True)
                    ins.then_inc(gates_ready, 1)

                def forget_sums():
                    pe.wait_ge(f_v, F_V_DONE)
                    T.matmul(bank[4][0:HEADS, 0:SEQ], logf[:, 0, :], tri[:, :], start=True, stop=False)
                    T.matmul(bank[4][0:HEADS, P:SEQ], logf[:, 1, :], tri[:, 0:P], start=False, stop=True)\
                        .then_inc(c_ready, 1)

                def scores(h):
                    if h == 0:
                        pe.wait_ge(c_loaded, 64)
                    if h % 2 == 0:
                        pe.wait_ge(z_evac, 10 + h // 2)
                    if h >= 2:
                        pe.wait_ge(l_done, 2 * h - 2)
                    rows = slice(64 * (h % 2), 64 * (h % 2) + 64)
                    pair = slice(32 * (h % 3), 32 * (h % 3) + 2)
                    S = bank[6 + h % 2]
                    for t in range(2):
                        q = slice(t * P, (t + 1) * P)
                        n = (t + 1) * P
                        dst = S[:, t * P:t * P + n]
                        T.matmul(dst, qT[rows, h // 2, q], kT[rows, h // 2, 0:n], start=True, stop=False)
                        ins = T.matmul(dst, cq[pair, h // 3, q], ck[pair, h // 3, 0:n], start=False, stop=True)
                    ins.then_inc(s_ready, 1)

                def turn_probs(h):
                    pe.wait_ge(pn_done, 2 * h + 2)
                    if h == 0:
                        pe.wait_ge(c_evac, 2)
                    else:
                        pe.wait_ge(pt_evac, h)
                    for b in range(3):
                        ins = turn(bank[4][:, b * P:(b + 1) * P], prob[h % 2][:, b * P:(b + 1) * P])
                    ins.then_inc(pt_ready, 1)

                def values(h):
                    pe.wait_ge(pt_evac, h + 1)
                    if h % 2 == 0 and h:
                        pe.wait_ge(ob_evac, h // 2)
                    rows = slice(64 * (h % 2), 64 * (h % 2) + 64)
                    cols = slice(64 * h, 64 * h + 64)
                    pT = probT[h % 2]
                    T.matmul(bank[5][rows, 0:P], vv[:, 0, cols], pT[:, 0:P], start=True, stop=True)
                    T.matmul(bank[5][rows, P:SEQ], vv[:, 0, cols], pT[:, P:2 * P], start=True, stop=False)
                    T.matmul(bank[5][rows, P:SEQ], vv[:, 1, cols], pT[:, 2 * P:], start=False, stop=True)\
                        .then_inc(pv_done, 1)

                def glu():
                    pe.wait_ge(ys_gelu, 1)
                    for m in range(2):
                        for k in range(2):
                            ins = T.matmul(bank[2][:, m * SEQ:(m + 1) * SEQ], wglu[:, k, m * P:(m + 1) * P], gs[:, k, :],
                                           start=k == 0, stop=k == 1)
                    ins.then_inc(glu_ready, 1)

                def square_sums(g, n, tiles_before):
                    pe.wait_ge(o_sq, tiles_before + n)
                    if g == 0:
                        pe.wait_ge(glu_sig, 1)
                    else:
                        pe.wait_ge(gstd_done, g)
                    for t in range(TT):
                        for k in range(n):
                            ins = T.matmul(bank[2][:, t:t + 1], squared[g][:, k, t * P:(t + 1) * P], ones[:, 0:1],
                                           start=k == 0, stop=k == n - 1)
                    ins.then_inc(ss_ready, 1)

                def proj_free(g, q):
                    n = 4 * g + q
                    if g == 2 and q >= 2:
                        pe.wait_ge(l_done, 2 * HEADS)
                    elif n < 2:
                        pe.wait_ge(z_evac, 17 + n)
                    elif n == 2:
                        pe.wait_ge(gate_sig, 6)
                    else:
                        pe.wait_ge(proj_evac, n - 2)

                def proj_part(g, q, tile, m, half, first, last):
                    hi, lo = piece(whi, MIX_BASE + m, 2, DM), piece(wlo, MIX_BASE + m, 2, DM)
                    tok, col = slice((q // 2) * P, (q // 2 + 1) * P), slice((q % 2) * 512, (q % 2 + 1) * 512)
                    a = tile % ACT_TILES
                    return mm3(bank[proj_bank(g, q)][:, :], act_hi[:, a, tok], act_lo[:, a, tok], hi[:, half, col],
                               lo[:, half, col], first, last)

                def project_s5(qs):
                    pe.wait_ge(o_lo, 2)
                    pe.wait_ge(lo_done, used(L, MIX_BASE + 9))
                    for q in qs:
                        proj_free(0, q)
                        proj_part(0, q, 0, 9, 0, True, False)
                        proj_part(0, q, 1, 9, 1, False, True).then_inc(proj_ready if q < 3 else pieces_used, 1)

                def project_rg_begin():
                    pe.wait_ge(o_lo, 4)
                    pe.wait_ge(lo_done, used(L, MIX_BASE + 10))
                    for q in range(3):
                        proj_free(1, q)
                        proj_part(1, q, 2, 10, 0, True, False)
                        proj_part(1, q, 3, 10, 1, False, False)

                def project_rg_end():
                    pe.wait_ge(o_lo, 5)
                    pe.wait_ge(lo_done, used(L, MIX_BASE + 11))
                    for q in range(3):
                        proj_part(1, q, 4, 11, 0, False, True).then_inc(proj_ready, 1)
                    proj_free(1, 3)
                    proj_part(1, 3, 2, 10, 0, True, False)
                    proj_part(1, 3, 3, 10, 1, False, False)
                    proj_part(1, 3, 4, 11, 0, False, True).then_inc(pieces_used, 1)

                def project_attention():
                    for tile, m, half, qs in ((5, 11, 1, (0, 1)), (6, 12, 0, (0, 1)), (7, 12, 1, (0, 1)),
                                              (5, 11, 1, (2, 3)), (6, 12, 0, (2, 3)), (7, 12, 1, (2, 3))):
                        pe.wait_ge(o_lo, tile + 1)
                        pe.wait_ge(lo_done, used(L, MIX_BASE + m))
                        for q in qs:
                            if tile == 5:
                                proj_free(2, q)
                            ins = proj_part(2, q, tile, m, half, tile == 5, tile == 7)
                            if tile == 7:
                                ins.then_inc(proj_ready if q < 3 else pieces_used, 1)
                            elif tile == 5 and q == 3:
                                ins.then_inc(pieces_used, 1)

                pe.wait_ge(xT_lo_done, 2)
                z_event(0)
                turn_rows(0, 1)
                z_event(2)
                pe.wait_ge(xT_lo_done, 4)
                z_event(1)
                z_event(3)
                pe.wait_ge(tab_step, TAB_MATS)
                for q in range(2):
                    for r in range(2):
                        ins = turn(bank[7][:, (2 * q + r) * P:(2 * q + r + 1) * P],
                                   bexp[:, r, 4 * q:4 * q + 4, :].rearrange("p a b -> p (a b)"))
                ins.then_inc(bc_turned, 1)
                for q in range(2):
                    for r in range(2):
                        ins = turn(bank[6][:, (2 * q + r) * P:(2 * q + r + 1) * P],
                                   cexp[:, q, r, :, :].rearrange("p a b -> p (a b)"))
                ins.then_inc(bc_turned, 1)
                z_event(4)
                z_event(5)
                bu(0)
                z_event(6)
                bu(1)
                z_event(7)
                y(0)
                bu(2)
                z_event(8)
                y(1)
                bu(3)
                forget_sums()
                z_event(9)
                y(2)
                bu(4)
                z_event(10)
                y(3)
                bu(5)
                scores(0)
                z_event(11)
                y(4)
                bu(6)
                scores(1)
                z_event(12)
                y(5)
                bu(7)
                turn_probs(0)
                z_event(13)
                y(6)
                values(0)
                scores(2)
                turn_probs(1)
                gates(0)
                z_event(14)
                y(7)
                values(1)
                scores(3)
                gates(1)
                z_event(15)
                turn_probs(2)
                scores(4)
                gates(2)
                z_event(16)
                values(2)
                turn_probs(3)
                glu()
                z_event(17)
                values(3)
                scores(5)
                square_sums(0, 2, 0)
                project_s5((0, 1))
                turn_probs(4)
                project_s5((2, 3))
                values(4)
                turn_probs(5)
                values(5)
                square_sums(1, 3, 2)
                project_rg_begin()
                project_rg_end()
                square_sums(2, 3, 5)
                project_attention()
                turn_rows(1, 0)
                turn_rows(1, 1)

                ffn(1)
                turn_rows(2, 1)
                pe.drain().then_inc(layer_arrived, 1)


def build(nc, shapes, out_shape):
    w = {}
    for name, shape in shapes.items():
        w[name] = nc.dram_tensor(f"in_{name}", shape, F32, kind="ExternalInput").ap()
    out = nc.dram_tensor("out", out_shape, F32, kind="ExternalOutput").ap()
    trunk(nc, w.pop("x"), w, out)


def kernel(**inputs):
    import numpy as np
    from concourse import bacc
    from concourse.bass_utils import run_bass_kernel_spmd

    nc = bacc.Bacc("TRN2", target_bir_lowering=False, num_devices=1)
    arrays = {name: np.ascontiguousarray(a) for name, a in inputs.items()}
    build(nc, {name: a.shape for name, a in arrays.items()}, arrays["x"].shape)
    result = run_bass_kernel_spmd(nc, [{f"in_{name}": a for name, a in arrays.items()}], core_ids=[0])
    return result.results[0]["out"]
```
